# Optimizing a Trainium2 kernel written in Bass

```python
import jax, jax.numpy as jnp
from jax import lax
import numpy as np

D_MODEL = 1024
BATCH = 1
SEQ = 512
DEPTH = 1

CONV_CH = D_MODEL
CONV_WIDTH = 31
HEAD_DIM = 64
N_Q_HEADS = D_MODEL // HEAD_DIM
N_KV_HEADS = N_Q_HEADS // 8
GROUP = N_Q_HEADS // N_KV_HEADS
WINDOW = 128
ROT_DIM = HEAD_DIM // 4
ROPE_THETA = 500000.0
W_CONV_COLS = 2 * CONV_CH
W_Q_COLS = N_Q_HEADS * HEAD_DIM
W_KV_COLS = N_KV_HEADS * HEAD_DIM
W_GATE_COLS = 2 * D_MODEL
IN_COLS = W_CONV_COLS + W_Q_COLS + 2 * W_KV_COLS + W_GATE_COLS
N_EXPERTS = 32
TOP_K = 4
D_EXPERT = D_MODEL
SWIGLU_LIMIT = 7.0
SWIGLU_ALPHA = 1.702
EXPERT_BLOCK = 128
RMS_EPS = 1e-5
LN_EPS = 1e-5

kernel_name = "hybrid_conformer_swa_sink_moe_block"

F32 = jnp.float32

def rms_norm(x, g):
    xf = x.astype(F32)
    y = xf * lax.rsqrt(jnp.mean(xf * xf, axis=-1, keepdims=True) + RMS_EPS)
    return (y * g.astype(F32)).astype(x.dtype)

def layer_norm(x, g, b):
    xf = x.astype(F32)
    mu = jnp.mean(xf, axis=-1, keepdims=True)
    var = jnp.mean(jnp.square(xf - mu), axis=-1, keepdims=True)
    y = (xf - mu) * lax.rsqrt(var + LN_EPS)
    return (y * g.astype(F32) + b.astype(F32)).astype(x.dtype)

def partial_rotary(x, positions):
    inv_freq = ROPE_THETA ** (-jnp.arange(0, ROT_DIM, 2, dtype=F32) / ROT_DIM)
    ang = positions.astype(F32)[..., None] * inv_freq
    cos = jnp.cos(ang)[:, :, None, :]
    sin = jnp.sin(ang)[:, :, None, :]
    xr = x[..., :ROT_DIM].astype(F32)
    x1, x2 = xr[..., : ROT_DIM // 2], xr[..., ROT_DIM // 2:]
    rot = jnp.concatenate([x1 * cos - x2 * sin, x2 * cos + x1 * sin], axis=-1)
    return jnp.concatenate([rot.astype(x.dtype), x[..., ROT_DIM:]], axis=-1)

def conformer_conv_branch(a, w_dw, b_dw, g_ln, b_ln, w_proj):
    val, gate = jnp.split(a, 2, axis=-1)
    c = val * jax.nn.sigmoid(gate)
    c = lax.conv_general_dilated(
        c, w_dw[:, None, :], window_strides=(1,),
        padding=[(CONV_WIDTH - 1, 0)],
        dimension_numbers=("NWC", "WIO", "NWC"),
        feature_group_count=CONV_CH) + b_dw
    c = layer_norm(c, g_ln, b_ln)
    c = jax.nn.silu(c)
    return c @ w_proj

def sliding_window_sink_attention(q, k, v, sinks):
    B, S = q.shape[0], q.shape[1]
    nb = S // WINDOW
    qb = q.reshape(B, nb, WINDOW, N_KV_HEADS, GROUP, HEAD_DIM)
    kb = k.reshape(B, nb, WINDOW, N_KV_HEADS, HEAD_DIM)
    vb = v.reshape(B, nb, WINDOW, N_KV_HEADS, HEAD_DIM)
    pad = jnp.zeros_like(kb[:, :1])
    kk = jnp.concatenate([jnp.concatenate([pad, kb[:, :-1]], axis=1), kb], axis=2)
    vv = jnp.concatenate([jnp.concatenate([pad, vb[:, :-1]], axis=1), vb], axis=2)
    scale = HEAD_DIM ** -0.5
    s = jnp.einsum("bnqhgd,bnkhd->bnhgqk", qb, kk, preferred_element_type=F32) * scale
    q_idx = jnp.arange(WINDOW)[:, None] + WINDOW
    k_idx = jnp.arange(2 * WINDOW)[None, :]
    rel = q_idx - k_idx
    band = (rel >= 0) & (rel < WINDOW)
    first = (jnp.arange(nb)[:, None, None] > 0) | (k_idx[None] >= WINDOW)
    mask = band[None] & first
    s = jnp.where(mask[None, :, None, None], s, -jnp.inf)
    sink = jnp.broadcast_to(sinks.astype(F32).reshape(1, 1, N_KV_HEADS, GROUP, 1, 1),
                            s.shape[:-1] + (1,))
    p = jax.nn.softmax(jnp.concatenate([s, sink], axis=-1), axis=-1)[..., :-1]
    o = jnp.einsum("bnhgqk,bnkhd->bnqhgd", p.astype(vv.dtype), vv)
    return o.reshape(B, S, N_Q_HEADS * HEAD_DIM)

def moe_ffn(u, w_router, b_router, w_mlp1, b_mlp1, w_mlp2, b_mlp2):
    B, S, D = u.shape
    t = u.reshape(-1, D)
    T = t.shape[0]
    n_assign = T * TOP_K
    logits = (t @ w_router + b_router).astype(F32)
    top_val, top_idx = lax.top_k(logits, TOP_K)
    gate = jax.nn.softmax(top_val, axis=-1)
    flat_e = top_idx.reshape(-1)
    flat_tok = jnp.arange(n_assign, dtype=jnp.int32) // TOP_K
    flat_g = gate.reshape(-1)
    order = jnp.argsort(flat_e)
    se = flat_e[order]
    counts = jnp.bincount(flat_e, length=N_EXPERTS)
    padded = (counts + EXPERT_BLOCK - 1) // EXPERT_BLOCK * EXPERT_BLOCK
    starts = jnp.cumsum(counts) - counts
    pstarts = jnp.cumsum(padded) - padded
    dest = pstarts[se] + jnp.arange(n_assign) - starts[se]
    n_blk = (n_assign + EXPERT_BLOCK - 1) // EXPERT_BLOCK + N_EXPERTS
    n_rows = n_blk * EXPERT_BLOCK
    row_tok = jnp.zeros((n_rows,), jnp.int32).at[dest].set(flat_tok[order])
    row_gate = jnp.zeros((n_rows,), F32).at[dest].set(flat_g[order])
    pends = jnp.cumsum(padded)
    blk_start = jnp.arange(n_blk) * EXPERT_BLOCK
    blk_e = jnp.minimum(jnp.sum(blk_start[:, None] >= pends[None, :], axis=1), N_EXPERTS - 1)
    xs = t[row_tok].reshape(n_blk, EXPERT_BLOCK, D)

    def expert_block(args):
        xb, e = args
        h = xb @ w_mlp1[e] + b_mlp1[e]
        glu, lin = jnp.split(h, 2, axis=-1)
        glu = jnp.minimum(glu, SWIGLU_LIMIT)
        lin = jnp.clip(lin, -SWIGLU_LIMIT, SWIGLU_LIMIT)
        a = glu * jax.nn.sigmoid(SWIGLU_ALPHA * glu) * (lin + 1)
        return a @ w_mlp2[e] + b_mlp2[e]

    ys = lax.map(expert_block, (xs, blk_e)).reshape(n_rows, D)
    out = jnp.zeros((T, D), u.dtype).at[row_tok].add(ys * row_gate[:, None].astype(ys.dtype))
    return out.reshape(B, S, D)

def setup_inputs(seed: int = 0) -> dict:
    key = jax.random.key(seed)
    ks = jax.random.split(key, 20)
    L, D, C, E, F = DEPTH, D_MODEL, CONV_CH, N_EXPERTS, D_EXPERT
    nrm = lambda k, shape, fan: jax.random.normal(k, shape, F32) * (fan ** -0.5)
    x = jax.random.normal(ks[0], (BATCH, SEQ, D), F32)
    positions = jnp.broadcast_to(jnp.arange(SEQ, dtype=jnp.int32), (BATCH, SEQ))
    return {
        "x": x,
        "positions": positions,
        "g_mix_norm": 1.0 + 0.02 * jax.random.normal(ks[1], (L, D), F32),
        "w_in": nrm(ks[2], (L, D, IN_COLS), D),
        "w_dw": nrm(ks[3], (L, CONV_WIDTH, C), CONV_WIDTH),
        "b_dw": 0.01 * jax.random.normal(ks[4], (L, C), F32),
        "g_conv_ln": 1.0 + 0.02 * jax.random.normal(ks[5], (L, C), F32),
        "b_conv_ln": 0.01 * jax.random.normal(ks[6], (L, C), F32),
        "w_conv_out": nrm(ks[7], (L, C, D), C),
        "attn_sinks": 0.5 * jax.random.normal(ks[8], (L, N_Q_HEADS), F32),
        "w_attn_out": nrm(ks[9], (L, N_Q_HEADS * HEAD_DIM, D), N_Q_HEADS * HEAD_DIM),
        "w_out": nrm(ks[10], (L, D, D), D),
        "g_ffn_norm": 1.0 + 0.02 * jax.random.normal(ks[11], (L, D), F32),
        "w_router": nrm(ks[12], (L, D, E), D),
        "b_router": 0.01 * jax.random.normal(ks[13], (L, E), F32),
        "w_mlp1": nrm(ks[14], (L, E, D, 2 * F), D),
        "b_mlp1": 0.01 * jax.random.normal(ks[15], (L, E, 2 * F), F32),
        "w_mlp2": nrm(ks[16], (L, E, F, D), F),
        "b_mlp2": 0.01 * jax.random.normal(ks[17], (L, E, D), F32),
        "g_final": 1.0 + 0.02 * jax.random.normal(ks[18], (D,), F32),
    }

def reference(x, positions, g_mix_norm, w_in, w_dw, b_dw, g_conv_ln, b_conv_ln, w_conv_out,
              attn_sinks, w_attn_out, w_out, g_ffn_norm, w_router, b_router,
              w_mlp1, b_mlp1, w_mlp2, b_mlp2, g_final):
    B, S, D = x.shape
    h = x
    split_at = np.cumsum([W_CONV_COLS, W_Q_COLS, W_KV_COLS, W_KV_COLS]).tolist()
    for l in range(DEPTH):
        u = rms_norm(h, g_mix_norm[l])
        proj = u @ w_in[l]
        a_conv, q, k, v, gates = jnp.split(proj, split_at, axis=-1)
        y_conv = conformer_conv_branch(a_conv, w_dw[l], b_dw[l], g_conv_ln[l],
                                       b_conv_ln[l], w_conv_out[l])
        q = partial_rotary(q.reshape(B, S, N_Q_HEADS, HEAD_DIM), positions)
        k = partial_rotary(k.reshape(B, S, N_KV_HEADS, HEAD_DIM), positions)
        v = v.reshape(B, S, N_KV_HEADS, HEAD_DIM)
        y_attn = sliding_window_sink_attention(q, k, v, attn_sinks[l]) @ w_attn_out[l]
        g_conv, g_attn = jnp.split(jax.nn.sigmoid(gates), 2, axis=-1)
        h = h + (g_conv * y_conv + g_attn * y_attn) @ w_out[l]
        u2 = rms_norm(h, g_ffn_norm[l])
        h = h + moe_ffn(u2, w_router[l], b_router[l], w_mlp1[l], b_mlp1[l],
                        w_mlp2[l], b_mlp2[l])
    return rms_norm(h, g_final)


_drawn_inputs = setup_inputs


def setup_inputs(seed=0):
    import zlib

    import numpy as np

    out = dict(_drawn_inputs(seed))
    spreads = {}
    factors = {'b_conv_ln': 2.803, 'attn_sinks': 5.901, 'b_mlp1': 8.0, 'b_mlp2': 8.0, 'g_final': 2.906}
    for name, (base, spread) in spreads.items():
        noise = np.random.default_rng([zlib.crc32(name.encode()), seed]).standard_normal(out[name].shape)
        drawn = base * np.exp(spread * noise) if base else spread * noise
        out[name] = __import__('jax').numpy.asarray(drawn.astype(out[name].dtype))
    for name, factor in factors.items():
        out[name] = (out[name] * factor).astype(out[name].dtype)
    return out
```

```python
from contextlib import ExitStack

import numpy as np

import concourse.bass as bass
from concourse import mybir

F32 = mybir.dt.float32
F32R = mybir.dt.float32r
BF16 = mybir.dt.bfloat16
I32 = mybir.dt.int32
ALU = mybir.AluOpType
ACT = mybir.ActivationFunctionType
AX = mybir.AxisListType

P = 128
D = 1024
SEQ = 512
TT = SEQ // P
KB = D // P
TAPS = 31
HALO = TAPS - 1
CW = SEQ + HALO
HEADS = 16
KV = 2
HD = 64
WIN = 128
SCALE = HD ** -0.5
EPS = 1e-5
E = 32
TOPK = 4
CAP = 96
G = 32
NG = CAP // G
FC = 256
LIMIT = 7.0
ALPHA = 1.702
MORE = (SEQ * TOPK) // CAP
NSLOT = 4
LIST = 3
I_MEAN, I_VAR = 11, 14
NU = 16

C_CONV, C_Q, C_KV, C_GATE, C_COUT, C_AOUT, C_WOUT, N_CHUNK = 0, 16, 24, 28, 44, 52, 60, 68
SKIP = 27


def used(n):
    return n + 1 if isinstance(n, int) and n < SKIP else n


def loads(n):
    return n // NSLOT + 1 - (n > SKIP and n % NSLOT == SKIP % NSLOT)


def upper(t, n):
    return (t.hi_early if n < C_COUT else t.hi_late)[(used(n) - 1) % 2]


K_ID, K_MEAN, K_ONE, K_ROT, K_MASK = 0, 128, 256, 384, 512
K_FREQ = K_MASK + 512
K_HALFPI = K_FREQ + 1
K_PAD = K_HALFPI + 1
K_ROW = K_PAD + NG
K_P = K_ROW + NG
K_E = K_P + 1
K_W = K_E + E
B_TRI, B_ONE, B_SLOT = 0, 128, 256
HOT = NG * P + CAP
B_TOK = B_SLOT + HOT
B_W = B_TOK + TT * 3
V_DW, V_BDW, V_GLN, V_BLN, V_GMIX, V_BR = 0, 248, 256, 264, 272, 280
V_W = 281

TWO_PI = 2.0 * np.pi
PI_A = 6.28125
PI_B = float(np.floor((TWO_PI - PI_A) * 2**20) / 2**20)
PI_C = float(TWO_PI - PI_A - PI_B)
ROUND = 1.5 * 2.0**23
MASKED = -1e30
UNROUTED = 4096.0


class Tensors:
    pass


class Chain:

    def __init__(self, eng, sem):
        self.eng, self.sem, self.n = eng, sem, 0

    def add(self, ins):
        ins.then_inc(self.sem, 1)
        self.n += 1

    def sync(self, back=0, base=0):
        self.eng.wait_ge(self.sem, base + self.n - back)

    def link(self, ins, base=0):
        self.add(ins)
        self.sync(0, base)


def at(ap3, i):
    return ap3[:, bass.ds(i, 1), :].rearrange("p a n -> p (a n)")


def halves(ap, n):
    return ap.rearrange("p (a n) -> p a n", n=n)


def heads_of(ap, u):
    hp, blk = (u // 8) * 4 + (u % 2) * 2, (u // 2) % 4
    return ap[:, hp:hp + 2, blk * WIN:(blk + 1) * WIN]


def dense_half(nc, t):
    bank = t.bank
    ident = t.kf[:, K_ID:K_ID + P]
    eps = t.eps[:, 0:1]

    with nc.Block() as block:

        @block.sync
        def _(sp):
            sp.dma_start(t.kf[:, :], t.d_kf).then_inc(t.s_const, 16)
            for q in range(4):
                sp.dma_start(t.xT[:, 2 * q:2 * q + 2, :], t.d_xT[:, 2 * q:2 * q + 2, :]).then_inc(t.s_xT[q], 16)
            for s in range(NSLOT):
                sp.dma_start(t.wring[:, s, :], t.d_dense[s]).then_inc(t.s_w[s], 16)
            with sp.Fori(1, C_KV // NSLOT) as r:
                for s in range(NSLOT):
                    sp.wait_ge(t.s_prod, (r - 1) * NSLOT + s + 1)
                    sp.dma_start(t.wring[:, s, :], t.d_dense[bass.ds(r * NSLOT + s, 1)].rearrange("a p n -> (a p) n")).then_inc(t.s_w[s], 16)
            for n in range(C_KV, C_GATE + NSLOT):
                if n != SKIP:
                    if n - NSLOT != SKIP:
                        sp.wait_ge(t.s_prod, used(n - NSLOT))
                    sp.dma_start(t.wring[:, n % NSLOT, :], t.d_dense[n]).then_inc(t.s_w[n % NSLOT], 16)
            with sp.Fori(C_GATE // NSLOT + 1, N_CHUNK // NSLOT) as r:
                for s in range(NSLOT):
                    sp.wait_ge(t.s_prod, (r - 1) * NSLOT + s)
                    sp.dma_start(t.wring[:, s, :], t.d_dense[bass.ds(r * NSLOT + s, 1)].rearrange("a p n -> (a p) n")).then_inc(t.s_w[s], 16)
            sp.wait_ge(t.s_prod, used(C_WOUT - 1))
            sp.dma_start(t.h[:, :, :], t.d_x.rearrange("(a p) d -> p a d", p=P)).then_inc(t.s_x, 16)
            sp.wait_ge(t.s_merge, 2 * KB)
            for k in range(KB - 2):
                sp.dma_start(t.w1[:, k, :], t.d_w1[0, k * P:(k + 1) * P, :]).then_inc(t.s_w1[k], 16)
            for j in range(4):
                sp.dma_start(t.w2[:, j, :, :], t.d_w2[0, j * FC:(j + 1) * FC, :].rearrange("(a p) n -> p a n", p=P)).then_inc(t.s_w2[j], 16)
            sp.wait_ge(t.s_prod, used(N_CHUNK - 1))
            for k in range(KB - 2, KB):
                sp.dma_start(t.w1[:, k, :], t.d_w1[0, k * P:(k + 1) * P, :]).then_inc(t.s_w1[k], 16)
            for j in range(TT):
                sp.wait_ge(t.s_u2, j + 1)
                sp.dma_start(t.d_u2[j * P:(j + 1) * P, :], t.u2[:, j, :]).then_inc(t.s_u2out, 16)
            sp.wait_ge(t.s_list, 1)
            sp.dma_start(t.d_list, t.listcol[:, :]).then_inc(t.s_listout, 16)
            sp.wait_ge(t.s_listout, 16)
            sp.dma_start(t.lists[:, :], t.d_list.rearrange("p c -> (p c)").unsqueeze(0)).then_inc(t.s_listin, 16)
            for j in range(TT):
                sp.wait_ge(t.s_acc, 2 * j + 2)
                sp.dma_start(t.d_acc[j * P:(j + 1) * P, :], t.h[:, j, :]).then_inc(t.s_accout, 16)
            sp.wait_ge(t.s_listin, 16)
            sp.wait_ge(t.s_u2out, 16 * TT)
            sp.wait_ge(t.s_accout, 16 * TT)

        @block.gpsimd
        def _(pool):
            pool.memset(t.cT[:, :, 0:HALO], 0.0).then_inc(t.s_zero, 1)
            pool.memset(t.kT[:, :, 0:WIN], 0.0).then_inc(t.s_zero, 1)
            pool.memset(t.v[:, 0, :], 0.0).then_inc(t.s_zero, 1)
            def zero_rows():
                pool.wait_ge(t.s_rope, 2)
                pool.memset(t.zrow[:, :], 0.0).then_inc(t.s_zero, 1)
                pool.wait_ge(t.s_zero, 4)
                pool.dma_start(t.d_acc[SEQ:SEQ + P, :], t.zrow[:, :]).then_inc(t.s_scat, 48)

            def weight_rest(slot, hi, count):
                pool.wait_ge(t.s_whi, count)
                pool.tensor_tensor(t.wlo[:, slot, :], t.wring[:, slot, :], hi.bitcast(F32), ALU.subtract).then_inc(t.s_wlo, 1)

            def rest(x, hi, lo, k, count):
                pool.wait_ge(t.s_hi, count)
                pool.tensor_tensor(lo[:, k, :], x[:, k, :], hi[:, k, :].bitcast(F32), ALU.subtract).then_inc(t.s_lo, 1)

            for n in range(2):
                weight_rest(n, upper(t, n), n + 1)
            for k in range(KB):
                rest(t.uT, t.u_hi, t.u_lo, k, k + 1)
            zero_rows()
            for n in range(2, NSLOT):
                weight_rest(n, upper(t, n), n + 1)
            with pool.Fori(1, C_KV // NSLOT) as r:
                for s in range(NSLOT):
                    weight_rest(s, upper(t, s), r * NSLOT + s + 1)
            for n in range(C_KV, C_COUT):
                if n != SKIP:
                    weight_rest(n % NSLOT, upper(t, n), used(n))
            for k in range(KB):
                rest(t.cv, t.cv_hi, t.cv_lo, k, KB + k + 1)
            for n in range(C_COUT, C_AOUT + 2):
                weight_rest(n % NSLOT, upper(t, n), used(n))
            for k in range(KB):
                n = C_AOUT + 2 + k
                weight_rest(n % NSLOT, upper(t, n), used(n))
                rest(t.mix, t.mix_hi, t.mix_lo, k, 2 * KB + k + 1)
            for n in range(C_WOUT + 2, N_CHUNK):
                weight_rest(n % NSLOT, upper(t, n), used(n))

        @block.scalar
        def _(act):
            act.dma_start(t.kb32[:, :], t.d_kb).then_inc(t.s_const, 16)
            act.dma_start(t.chan[:, :], t.d_chan).then_inc(t.s_const, 16)
            act.dma_start(t.pos_i[:, :], t.d_pos.partition_broadcast(P)).then_inc(t.s_const, 16)
            act.dma_start(t.sinks[:, :], t.d_sinks.partition_broadcast(P)).then_inc(t.s_const, 16)
            act.dma_start(t.wr[:, :], t.d_wr).then_inc(t.s_const, 16)

            def weight_upper(slot, hi, loaded):
                act.wait_ge(t.s_w[slot], loaded)
                act.activation(hi, t.wring[:, slot, :], ACT.Copy).then_inc(t.s_whi, 1)

            for k in range(0, KB, 2):
                act.wait_ge(t.s_xT[k // 2], 16)
                act.activation(t.uT[:, k, :], t.xT[:, k, :], ACT.Square).then_inc(t.s_sq, 1)
            for n in range(2):
                weight_upper(n, upper(t, n), 16)
            act.wait_ge(t.s_stat, 1)
            act.wait_ge(t.s_eps, 1)
            act.activation(t.rstd[:, :], bank[7][:, :], ACT.Sqrt, bias=eps).then_inc(t.s_root, 1)
            for k in range(KB):
                act.wait_ge(t.s_uT, k + 1)
                act.activation(t.u_hi[:, k, :], t.uT[:, k, :], ACT.Copy).then_inc(t.s_hi, 1)
            act.wait_ge(t.s_ang, 2)
            act.activation(t.sin[:, :], t.ang[:, :], ACT.Sin).then_inc(t.s_rope, 1)
            act.activation(t.cos[:, :], t.cos[:, :], ACT.Sin, bias=t.kf[:, K_HALFPI:K_HALFPI + 1], scale=-1.0).then_inc(t.s_rope, 1)
            with act.Fori(0, C_Q // NSLOT) as r:
                for s in range(NSLOT):
                    act.wait_ge(t.s_prod, r * 4 + s + 1)
                    if s % 2 == 0:
                        act.activation(t.cT[:, bass.ds(r * 2 + s // 2, 1), HALO:CW].rearrange("p a n -> p (a n)"), bank[s][:, :], ACT.Copy).then_inc(t.s_evac, 1)
                    else:
                        act.activation(at(t.gates, r * 2 + s // 2 + KB), bank[s][:, :], ACT.Sigmoid).then_inc(t.s_evac, 1)
                    weight_upper((s + 2) % 4, upper(t, s), (r + (s + 2) // 4) * 16 + 16)
            with act.Fori(0, KB // NSLOT) as r:
                for s in range(NSLOT):
                    act.wait_ge(t.s_prod, r * 4 + s + C_Q + 1)
                    act.activation(at(t.qT, r * 4 + s), bank[s][:, :], ACT.Copy).then_inc(t.s_evac, 1)
                    weight_upper((s + 2) % 4, upper(t, s), (r + C_Q // 4 + (s + 2) // 4) * 16 + 16)
            for n, out in ((C_KV, t.kT[:, 0, WIN:]), (C_KV + 1, t.kT[:, 1, WIN:]), (C_KV + 2, t.vT[:, :])):
                act.wait_ge(t.s_prod, n + 1)
                act.activation(out, bank[n % NSLOT][:, :], ACT.Copy).then_inc(t.s_evac, 1)
                m = n + 2 if n + 2 < SKIP else n + 3
                weight_upper(m % NSLOT, upper(t, m), 16 * loads(m))
            for n in range(C_GATE, C_COUT):
                i = n - C_GATE
                act.wait_ge(t.s_prod, used(n))
                if i >= KB:
                    act.wait_ge(t.s_gated, i - KB + 1)
                act.activation(t.gates[:, i, :], bank[n % NSLOT][:, :], ACT.Sigmoid).then_inc(t.s_evac, 1)
                if n + 2 < C_COUT:
                    weight_upper((n + 2) % NSLOT, upper(t, n + 2), 16 * loads(n + 2))
                if i == 0:
                    act.wait_ge(t.s_vt, 1)
                    act.activation(t.v[:, 1:, :], halves(bank[4][:, :], P), ACT.Copy).then_inc(t.s_v, 1)
                for k in range(4 * (i - I_MEAN), 4 * (i - I_MEAN) + 4) if i in (I_MEAN, I_MEAN + 1) else ():
                    act.wait_ge(t.s_cent, k + 1)
                    act.activation(t.xT[:, k, :], t.cv[:, k, :], ACT.Square).then_inc(t.s_lnsq, 1)
                if i == I_VAR:
                    act.wait_ge(t.s_stat, 3)
                    act.activation(t.rstd[:, :], bank[7][:, :], ACT.Sqrt, bias=eps).then_inc(t.s_root, 1)
                for k in range(KB) if i == I_VAR + 1 else ():
                    act.wait_ge(t.s_lnt, k + 1)
                    act.activation(t.xT[:, k, :], t.cv[:, k, :], ACT.Sigmoid, bias=t.chan[:, V_BLN + k:V_BLN + k + 1],
                                   scale=t.chan[:, V_GLN + k:V_GLN + k + 1]).then_inc(t.s_lns, 1)
            for k in range(KB):
                act.wait_ge(t.s_ln, k + 1)
                act.activation(t.cv_hi[:, k, :], t.cv[:, k, :], ACT.Copy).then_inc(t.s_hi, 1)
            act.wait_ge(t.s_rot, KB + KV)
            act.wait_ge(t.s_scat, 48)
            weight_upper(C_COUT % NSLOT, upper(t, C_COUT), 16 * loads(C_COUT))

            def exponentials(u):
                act.wait_ge(t.s_max, u + 1)
                for x in range(4):
                    act.activation(t.sm[:, u % 2, x, :], t.sm[:, u % 2, x, :], ACT.Exp, bias=t.negm[:, u, x:x + 1],
                                   scale=SCALE, accum_out=t.rsum[:, u, x:x + 1]).then_inc(t.s_exp, 1)
                act.activation(t.esink[:, u, :], t.esink[:, u, :], ACT.Exp).then_inc(t.s_exp, 1)

            exponentials(0)
            exponentials(1)
            for u in range(NU):
                act.wait_ge(t.s_pt, 2 * u + 1)
                if u:
                    act.wait_ge(t.s_pv, u)
                act.activation(t.pT[:, 0, :, :], halves(bank[4][:, :], P), ACT.Copy).then_inc(t.s_ept0, 1)
                act.wait_ge(t.s_pv, u + 1)
                act.activation(heads_of(t.o_hi, u), halves(bank[6][:, 0:2 * WIN], WIN), ACT.Copy).then_inc(t.s_eo, 1)
                if u + 2 < NU:
                    exponentials(u + 2)
                if u % 2 == 0:
                    n = C_COUT + u // 2 + 1
                    if u:
                        act.wait_ge(t.s_prod, used(n - 2))
                    weight_upper(n % NSLOT, upper(t, n), 16 * loads(n))
            n = C_AOUT + 1
            act.wait_ge(t.s_prod, used(n - 2))
            weight_upper(n % NSLOT, upper(t, n), 16 * loads(n))
            act.wait_ge(t.s_pt, 2 * NU)
            act.dma_start(t.gffn[:, :], t.d_gffn.partition_broadcast(P)).then_inc(t.s_late, 16)
            act.dma_start(t.b2[:, :], t.d_b2).then_inc(t.s_late, 16)
            for n in range(C_AOUT + 2, N_CHUNK):
                act.wait_ge(t.s_prod, used(n - 2))
                weight_upper(n % NSLOT, upper(t, n), 16 * loads(n))
                k = n - C_AOUT - 2
                if k < KB:
                    act.wait_ge(t.s_merge, KB + k + 1)
                    act.activation(t.mix_hi[:, k, :], t.mix[:, k, :], ACT.Copy).then_inc(t.s_hi, 1)
            for j in range(TT):
                act.wait_ge(t.s_h, 2 * j + 2)
                if j:
                    act.wait_ge(t.s_ss, j)
                act.activation(t.junk[:, :], t.h[:, j, :], ACT.Square, accum_out=t.ss[:, j:j + 1]).then_inc(t.s_ss, 1)
            act.wait_ge(t.s_ss, TT)
            act.activation(t.ss[:, :], t.ss[:, :], ACT.Sqrt, bias=eps, scale=1.0 / D).then_inc(t.s_root, 1)
            for j in range(TT):
                act.wait_ge(t.s_ut, 2 * j + 1)
                act.activation(t.u2T[:, 0:4, j * P:(j + 1) * P], halves(bank[2 * (j % 2)][:, :], P), ACT.Copy).then_inc(t.s_eut0, 1)
            act.wait_ge(t.s_top, 1)
            for j in range(TT):
                act.activation(t.gexp[:, j, :], t.logits[:, j, :], ACT.Exp, bias=t.nv1[:, j:j + 1]).then_inc(t.s_gexp, 1)

        @block.tensor
        def _(pe):
            def parts(out, lhs_hi, lhs_lo, rhs_hi, rhs_lo, start, stop):
                for i, (a, b) in enumerate(((lhs_hi, rhs_hi), (lhs_lo, rhs_hi), (lhs_hi, rhs_lo))):
                    mm = pe.matmul(out, a, b, start=start and i == 0, stop=stop and i == 2)
                return mm

            def product(out, s, hi, count, rhs_hi, rhs_lo, ks=range(KB), ready=False):
                pe.wait_ge(t.s_wlo, count)
                for k in ks:
                    if ready:
                        pe.wait_ge(t.s_lo, k + 1)
                    mm = parts(out, hi[:, k * P:(k + 1) * P], t.wlo[:, s, k * P:(k + 1) * P], rhs_hi[:, k, :], rhs_lo[:, k, :], k == 0, k == KB - 1)
                if KB - 1 in ks:
                    mm.then_inc(t.s_prod, 1)

            pe.wait_ge(t.s_const, 16 * 6)
            for k in range(KB):
                pe.wait_ge(t.s_sq if k % 2 == 0 else t.s_sqodd, k // 2 + 1)
                mm = pe.matmul(bank[7][:, :], t.kf[:, K_MEAN:K_MEAN + P], t.uT[:, k, :], start=(k == 0), stop=(k == KB - 1))
            mm.then_inc(t.s_stat, 1)

            for s in range(NSLOT):
                product(bank[s][:, :], s, upper(t, s), s + 1, t.u_hi, t.u_lo, ready=(s == 0))
            with pe.Fori(1, C_KV // NSLOT) as r:
                for s in range(NSLOT):
                    pe.wait_ge(t.s_evac, r * 4 + s - 3)
                    product(bank[s][:, :], s, upper(t, s), r * 4 + s + 1, t.u_hi, t.u_lo)
            for n in range(C_KV, SKIP):
                pe.wait_ge(t.s_evac, n - 3)
                product(bank[n % NSLOT][:, :], n % NSLOT, upper(t, n), used(n), t.u_hi, t.u_lo)
            for n in range(C_GATE, C_COUT):
                s, i = n % NSLOT, n - C_GATE
                if i == I_MEAN:
                    pe.wait_ge(t.s_conv, KB)
                    for k in range(KB):
                        mm = pe.matmul(bank[6][:, :], t.kf[:, K_MEAN:K_MEAN + P], t.cv[:, k, :], start=(k == 0), stop=(k == KB - 1))
                    mm.then_inc(t.s_stat, 1)
                if i == I_VAR:
                    for k in range(KB):
                        pe.wait_ge(t.s_lnsq, k + 1)
                        mm = pe.matmul(bank[7][:, :], t.kf[:, K_MEAN:K_MEAN + P], t.xT[:, k, :], start=(k == 0), stop=(k == KB - 1))
                    mm.then_inc(t.s_stat, 1)
                pe.wait_ge(t.s_evac, n - 3 if n < C_GATE + 3 else n - NSLOT)
                product(bank[s][:, :], s, upper(t, n), used(n), t.u_hi, t.u_lo)
                if i == 0:
                    pe.wait_ge(t.s_evac, SKIP)
                    for j in range(TT):
                        mm = pe.transpose(bank[4][:, j * P:(j + 1) * P], t.vT[:, j * P:(j + 1) * P], ident)
                    mm.then_inc(t.s_vt, 1)
                if i >= I_MEAN:
                    for j in range(2 * (i - I_MEAN), 2 * (i - I_MEAN) + 2):
                        src = t.qT[:, j, :] if j < KB else t.kT[:, j - KB, WIN:]
                        if j >= 2:
                            pe.wait_ge(t.s_rot, j - 1)
                        else:
                            pe.wait_ge(t.s_v, 1)
                        pe.matmul(bank[4 + j % 2][:, :], t.kf[:, K_ROT:K_ROT + P], src, start=True, stop=True).then_inc(t.s_swap, 1)

            def scores(u):
                hp, blk, kv = (u // 8) * 4 + (u % 2) * 2, (u // 2) % 4, u // 8
                if u == 0:
                    pe.wait_ge(t.s_evac, C_COUT - 1)
                    pe.wait_ge(t.s_rot, KB + KV)
                    pe.wait_ge(t.s_zero, 3)
                if u >= 2:
                    pe.wait_ge(t.s_masked, 2 * (u - 1))
                for x in range(2):
                    for half in range(2):
                        rows = slice(half * HD, half * HD + HD)
                        mm = pe.matmul(bank[2 * (u % 2) + half][:, x * 2 * WIN:(x + 1) * 2 * WIN], t.qT[rows, hp + x, blk * WIN:(blk + 1) * WIN],
                                       t.kT[rows, kv, blk * WIN:(blk + 2) * WIN], start=True, stop=True)
                mm.then_inc(t.s_score, 1)

            def turn_probs(u):
                pe.wait_ge(t.s_prob, u + 1)
                for kt in range(2):
                    if u:
                        pe.wait_ge((t.s_ept0, t.s_ept1)[kt], u)
                    for x in range(4):
                        mm = pe.transpose(bank[4 + kt][:, x * P:(x + 1) * P], t.sm[:, u % 2, x, kt * P:(kt + 1) * P], ident)
                    mm.then_inc(t.s_pt, 1)

            def values(u):
                blk, kv = (u // 2) % 4, u // 8
                pe.wait_ge(t.s_ept0, u + 1)
                pe.wait_ge(t.s_ept1, u + 1)
                if u:
                    pe.wait_ge(t.s_olo, u)
                for half in range(2):
                    for kt in range(2):
                        mm = pe.matmul(bank[6][half * HD:(half + 1) * HD, 0:2 * WIN], t.v[:, blk + kt, kv * HD:(kv + 1) * HD],
                                       t.pT[:, kt, 2 * half:2 * half + 2, :], start=(kt == 0), stop=(kt == 1))
                mm.then_inc(t.s_pv, 1)

            scores(0)
            scores(1)
            for u in range(NU):
                turn_probs(u)
                if u + 2 < NU:
                    scores(u + 2)
                n = C_COUT + u // 2
                if u == 0:
                    values(0)
                    pe.wait_ge(t.s_lo, 2 * KB)
                elif u % 2 == 0:
                    pe.wait_ge(t.s_merge, u // 2)
                product(bank[7][:, :], n % NSLOT, upper(t, n), used(n), t.cv_hi, t.cv_lo, ks=range(u % 2 * 4, u % 2 * 4 + 4))
                if u:
                    values(u)

            pe.wait_ge(t.s_masked, 2 * NU)
            pe.wait_ge(t.s_olo, NU)
            for n in range(C_AOUT, C_WOUT):
                if n >= C_AOUT + NSLOT:
                    pe.wait_ge(t.s_merge, KB + n - C_AOUT - NSLOT + 1)
                product(bank[n % NSLOT][:, :], n % NSLOT, upper(t, n), used(n), t.o_hi, t.o_lo)
            pe.wait_ge(t.s_merge, 2 * KB)
            for k in range(KB):
                n = C_WOUT + k
                pe.wait_ge(t.s_wlo, used(n))
                pe.wait_ge(t.s_lo, 2 * KB + k + 1)
                for j in range(TT):
                    for c in range(2):
                        tok, col = slice(j * P, (j + 1) * P), slice(c * SEQ, (c + 1) * SEQ)
                        mm = parts(bank[2 * j + c][:, :], t.mix_hi[:, k, tok], t.mix_lo[:, k, tok], upper(t, n)[:, col], t.wlo[:, n % NSLOT, col],
                                   k == 0, k == KB - 1)
                mm.then_inc(t.s_prod, 1)
            for j in range(TT):
                pe.wait_ge(t.s_u2, j + 1)
                if j == 0:
                    pe.wait_ge(t.s_h, 2 * TT)
                if j >= 2:
                    pe.wait_ge(t.s_eut0, j - 1)
                    pe.wait_ge(t.s_eut1, j - 1)
                for c in range(2):
                    for x in range(4):
                        k = 4 * c + x
                        mm = pe.transpose(bank[2 * (j % 2) + c][:, x * P:(x + 1) * P], t.u2[:, j, k * P:(k + 1) * P], ident)
                    mm.then_inc(t.s_ut, 1)
            pe.wait_ge(t.s_eut0, TT)
            pe.wait_ge(t.s_eut1, TT)
            for k in range(KB):
                for j in range(TT):
                    mm = pe.matmul(bank[4][E * j:E * (j + 1), 0:P], t.wr[:, k * E:(k + 1) * E], t.u2T[:, k, j * P:(j + 1) * P],
                                   start=(k == 0), stop=(k == KB - 1))
            mm.then_inc(t.s_route, 1)
            pe.wait_ge(t.s_lt, 1)
            pe.transpose(bank[5][:, 0:P], t.lT[:, :], ident).then_inc(t.s_route, 1)
            pe.wait_ge(t.s_sel, 1)
            selb = t.selb[:, :, :]
            pe.matmul(halves(bank[6][:, 0:TT * E], E), t.kb[:, B_TRI:B_TRI + P], selb, start=True, stop=False)
            for j in range(TT - 1):
                for i in range(j + 1, TT):
                    mm = pe.matmul(bank[6][:, i * E:(i + 1) * E], t.kb[:, B_ONE:B_ONE + P], t.selb[:, j, :], start=False, stop=(j == TT - 2))
            mm.then_inc(t.s_route, 1)
            for j in range(TT):
                mm = pe.matmul(bank[7][:, 0:E], t.kb[:, B_ONE:B_ONE + P], t.selb[:, j, :], start=(j == 0), stop=(j == TT - 1))
            mm.then_inc(t.s_route, 1)
            pe.wait_ge(t.s_gate, 1)
            pe.transpose(bank[5][:, P:2 * P], t.gate[:, :, :].rearrange("p a n -> p (a n)"), ident).then_inc(t.s_route, 1)
            pe.wait_ge(t.s_gT, 1)
            pe.wait_ge(t.s_late, 32)
            for j in range(TT):
                for c in range(2):
                    if j >= 2:
                        pe.wait_ge(t.s_acc, 2 * (j - 2) + c + 1)
                    pe.matmul(bank[2 * (j % 2) + c][:, :], t.gT[E * j:E * (j + 1), :], t.b2[E * j:E * (j + 1), c * SEQ:(c + 1) * SEQ],
                              start=True, stop=True, tile_position=(E * j, 0)).then_inc(t.s_bias, 1)
            pe.wait_ge(t.s_diag, 1)
            pe.matmul(bank[4][:, 0:P], t.kf[:, K_ONE:K_ONE + P], t.diag[:, :], start=True, stop=True).then_inc(t.s_first, 1)

        @block.vector
        def _(dve):
            step = Chain(dve, t.s_dve)
            dve.memset(t.eps[:, :], EPS).then_inc(t.s_eps, 1)
            for k in range(1, KB, 2):
                dve.wait_ge(t.s_xT[k // 2], 16)
                dve.tensor_tensor(t.uT[:, k, :], t.xT[:, k, :], t.xT[:, k, :], ALU.mult).then_inc(t.s_sqodd, 1)
            dve.wait_ge(t.s_const, 16 * 6)
            dve.wait_ge(t.s_root, 1)
            step.link(dve.reciprocal(t.rstd[:, :], t.rstd[:, :]))
            for k in range(KB):
                dve.scalar_tensor_tensor(t.uT[:, k, :], t.xT[:, k, :], t.chan[:, V_GMIX + k:V_GMIX + k + 1], t.rstd[:, :],
                                         ALU.mult, ALU.mult).then_inc(t.s_uT, 1)
            step.link(dve.tensor_copy(t.kb[:, :], t.kb32[:, :]))
            step.link(dve.tensor_copy(t.ang[:, :], t.pos_i[:, :]))
            step.link(dve.tensor_scalar(t.ang[:, :], t.ang[:, :], t.kf[:, K_FREQ:K_FREQ + 1], None, ALU.mult))
            step.link(dve.tensor_scalar(t.cos[:, :], t.ang[:, :], 1.0 / TWO_PI, ROUND, ALU.mult, ALU.add))
            step.link(dve.tensor_scalar(t.cos[:, :], t.cos[:, :], ROUND, None, ALU.subtract))
            for part in (PI_A, PI_B, PI_C):
                step.link(dve.scalar_tensor_tensor(t.ang[:, :], t.cos[:, :], -part, t.ang[:, :], ALU.mult, ALU.add))
            step.link(dve.tensor_scalar(t.ang[:, :], t.ang[:, :], 3.1415925, -3.1415925, ALU.min, ALU.max))
            dve.tensor_scalar(t.cos[:, :], t.ang[:, :], -1.0, None, ALU.mult).then_inc(t.s_ang, 1)
            dve.wait_ge(t.s_ang, 1)
            dve.tensor_tensor(t.cos[:, :], t.cos[:, :], t.ang[:, :], ALU.max).then_inc(t.s_ang, 1)
            dve.wait_ge(t.s_zero, 1)
            with dve.Fori(0, KB) as i:
                conv = Chain(dve, t.s_tap)
                base = i * (TAPS + 1)
                row = at(t.cv, i)

                def tap(k):
                    return t.cT[:, bass.ds(i, 1), k:k + SEQ].rearrange("p a n -> p (a n)")

                def weight(k):
                    return t.chan[:, bass.ds(i * TAPS + V_DW + k, 1)]

                dve.wait_ge(t.s_evac, i * 2 + 2)
                conv.link(dve.tensor_tensor(tap(HALO), tap(HALO), at(t.gates, i + KB), ALU.mult), base)
                conv.add(dve.tensor_scalar(row, tap(0), weight(0), t.chan[:, bass.ds(i + V_BDW, 1)], ALU.mult, ALU.add))
                conv.add(dve.tensor_scalar(t.odd[:, :], tap(1), weight(1), None, ALU.mult))
                for k in range(2, TAPS):
                    acc = t.odd[:, :] if k % 2 else row
                    conv.sync(1, base)
                    conv.add(dve.scalar_tensor_tensor(acc, tap(k), weight(k), acc, ALU.mult, ALU.add))
                conv.sync(0, base)
                assert conv.n == TAPS + 1
                dve.tensor_tensor(row, row, t.odd[:, :], ALU.add).then_inc(t.s_conv, 1)
                dve.wait_ge(t.s_conv, i + 1)
                dve.sem_inc(t.s_gated, 1)
            dve.wait_ge(t.s_stat, 2)
            for k in range(KB):
                dve.tensor_tensor(t.cv[:, k, :], t.cv[:, k, :], bank[6][:, :], ALU.subtract).then_inc(t.s_cent, 1)
            dve.wait_ge(t.s_rope, 2)
            dve.wait_ge(t.s_evac, C_KV + KV)
            for i in range(KB + KV):
                x = t.qT[:, i, :] if i < KB else t.kT[:, i - KB, WIN:]
                dve.wait_ge(t.s_swap, i + 1)
                step.add(dve.tensor_tensor(x, x, t.cos[:, :], ALU.mult))
                step.link(dve.tensor_tensor(t.odd[:, :], bank[4 + i % 2][:, :], t.sin[:, :], ALU.mult))
                dve.tensor_tensor(x, x, t.odd[:, :], ALU.add).then_inc(t.s_rot, 1)
                dve.wait_ge(t.s_rot, i + 1)
                if i == 2 * (I_VAR - I_MEAN) - 1:
                    dve.wait_ge(t.s_cent, KB)
                    dve.wait_ge(t.s_root, 2)
                    step.link(dve.reciprocal(t.rstd[:, :], t.rstd[:, :]))
                    for k in range(KB):
                        dve.tensor_tensor(t.cv[:, k, :], t.cv[:, k, :], t.rstd[:, :], ALU.mult).then_inc(t.s_lnt, 1)
            for k in range(KB):
                dve.wait_ge(t.s_lns, k + 1)
                step.add(dve.tensor_scalar(t.cv[:, k, :], t.cv[:, k, :], t.chan[:, V_GLN + k:V_GLN + k + 1],
                                           t.chan[:, V_BLN + k:V_BLN + k + 1], ALU.mult, ALU.add))
            for k in range(KB):
                step.sync(KB - 1 - k)
                dve.tensor_tensor(t.cv[:, k, :], t.cv[:, k, :], t.xT[:, k, :], ALU.mult).then_inc(t.s_ln, 1)

            def masked(u):
                blk = (u // 2) % 4
                mask = t.kf[:, K_MASK + 256 * (blk == 0):K_MASK + 256 * (blk == 0) + 256].unsqueeze(1).to_broadcast([P, 2, 2 * WIN])
                dve.wait_ge(t.s_score, u + 1)
                if u == 0:
                    dve.wait_ge(t.s_prod, used(C_COUT - 1))
                if u >= 2:
                    dve.wait_ge(t.s_pt, 2 * (u - 1))
                for half in range(2):
                    dve.tensor_tensor(t.sm[:, u % 2, 2 * half:2 * half + 2, :], halves(bank[2 * (u % 2) + half][:, :], 2 * WIN), mask,
                                      ALU.add).then_inc(t.s_masked, 1)
                dve.wait_ge(t.s_masked, 2 * (u + 1))
                mx, sinks = t.mx[:, u, :], t.sinks[:, 4 * (u // 8 * 2 + u % 2):4 * (u // 8 * 2 + u % 2) + 4]
                step.link(dve.tensor_reduce(mx, t.sm[:, u % 2, :, :], AX.X, ALU.max))
                step.link(dve.scalar_tensor_tensor(mx, mx, SCALE, sinks, ALU.mult, ALU.max))
                step.link(dve.tensor_scalar(t.negm[:, u, :], mx, -1.0, None, ALU.mult))
                dve.tensor_tensor(t.esink[:, u, :], sinks, t.negm[:, u, :], ALU.add).then_inc(t.s_max, 1)

            def output_rest(u):
                dve.wait_ge(t.s_eo, u + 1)
                dve.tensor_tensor(heads_of(t.o_lo, u), halves(bank[6][:, 0:2 * WIN], WIN), heads_of(t.o_hi, u).bitcast(F32), ALU.subtract).then_inc(t.s_olo, 1)

            def gate_conv(k):
                dve.wait_ge(t.s_prod, used(C_COUT + k))
                dve.tensor_tensor(t.mix[:, k, :], bank[7][:, :], t.gates[:, k, :], ALU.mult).then_inc(t.s_merge, 1)

            def probabilities(u):
                dve.wait_ge(t.s_exp, 5 * (u + 1))
                step.link(dve.tensor_tensor(t.rsum[:, u, :], t.rsum[:, u, :], t.esink[:, u, :], ALU.add))
                step.link(dve.reciprocal(t.rsum[:, u, :], t.rsum[:, u, :]))
                for x in range(4):
                    step.add(dve.tensor_scalar(t.sm[:, u % 2, x, :], t.sm[:, u % 2, x, :], t.rsum[:, u, x:x + 1], None, ALU.mult))
                step.sync()
                dve.sem_inc(t.s_prob, 1)

            masked(0)
            masked(1)
            probabilities(0)
            for u in range(NU):
                dve.wait_ge(t.s_pt, 2 * u + 2)
                if u:
                    dve.wait_ge(t.s_pv, u)
                dve.tensor_copy(t.pT[:, 1, :, :], halves(bank[5][:, :], P)).then_inc(t.s_ept1, 1)
                if u + 2 < NU:
                    masked(u + 2)
                if u + 1 < NU:
                    probabilities(u + 1)
                output_rest(u)
                if u % 2:
                    gate_conv(u // 2)
            dve.wait_ge(t.s_merge, KB)
            for k in range(KB):
                dve.wait_ge(t.s_prod, used(C_AOUT + k))
                step.link(dve.tensor_tensor(t.odd[:, :], bank[(C_AOUT + k) % NSLOT][:, :], t.gates[:, KB + k, :], ALU.mult))
                dve.tensor_tensor(t.mix[:, k, :], t.mix[:, k, :], t.odd[:, :], ALU.add).then_inc(t.s_merge, 1)
                dve.wait_ge(t.s_merge, KB + k + 1)
            dve.wait_ge(t.s_x, 16)
            dve.wait_ge(t.s_prod, used(N_CHUNK - 1))
            for j in range(TT):
                for c in range(2):
                    dve.tensor_tensor(t.h[:, j, c * SEQ:(c + 1) * SEQ], t.h[:, j, c * SEQ:(c + 1) * SEQ], bank[2 * j + c][:, :], ALU.add).then_inc(t.s_h, 1)
            dve.wait_ge(t.s_h, 2 * TT)
            dve.wait_ge(t.s_late, 32)
            dve.wait_ge(t.s_root, 3)
            step.link(dve.reciprocal(t.ss[:, :], t.ss[:, :]))
            for j in range(TT):
                dve.scalar_tensor_tensor(t.u2[:, j, :], t.h[:, j, :], t.ss[:, j:j + 1], t.gffn[:, :], ALU.mult, ALU.mult).then_inc(t.s_u2, 1)
            for j in range(TT):
                dve.wait_ge(t.s_ut, 2 * j + 2)
                dve.tensor_copy(t.u2T[:, 4:8, j * P:(j + 1) * P], halves(bank[2 * (j % 2) + 1][:, :], P)).then_inc(t.s_eut1, 1)
            dve.wait_ge(t.s_route, 1)
            dve.tensor_scalar(t.lT[:, :], bank[4][:, 0:P], t.chan[:, V_BR:V_BR + 1], None, ALU.add).then_inc(t.s_lt, 1)
            dve.wait_ge(t.s_route, 2)
            step.link(dve.tensor_copy(t.logits[:, :, :], halves(bank[5][:, 0:P], E)))
            for j in range(TT):
                step.add(dve.max(t.top[:, j, :], t.logits[:, j, :]))
            step.sync()
            dve.tensor_scalar(t.nv1[:, :].unsqueeze(2), t.top[:, :, 0:1], -1.0, None, ALU.mult).then_inc(t.s_top, 1)
            v4 = t.top[:, :, TOPK - 1:TOPK].to_broadcast([P, TT, E])
            step.add(dve.tensor_tensor(t.sel[:, :, :], t.logits[:, :, :], v4, ALU.is_gt))
            step.link(dve.tensor_tensor(t.tie[:, :, :], t.logits[:, :, :], v4, ALU.is_equal))
            step.link(dve.tensor_reduce(t.room[:, :], t.sel[:, :, :], AX.X, ALU.add))
            step.link(dve.tensor_scalar(t.room[:, :], t.room[:, :], -1.0, float(TOPK), ALU.mult, ALU.add))
            for j in range(TT):
                step.add(dve.tensor_tensor_scan(t.rank[:, j, :], t.kf[:, K_ONE:K_ONE + E], t.tie[:, j, :], 0.0, ALU.mult, ALU.add))
            step.sync()
            step.link(dve.tensor_tensor(t.rank[:, :, :], t.rank[:, :, :], t.room[:, :].unsqueeze(2).to_broadcast([P, TT, E]), ALU.is_le))
            step.link(dve.tensor_tensor(t.tie[:, :, :], t.tie[:, :, :], t.rank[:, :, :], ALU.mult))
            step.link(dve.tensor_tensor(t.sel[:, :, :], t.sel[:, :, :], t.tie[:, :, :], ALU.add))
            dve.tensor_copy(t.selb[:, :, :], t.sel[:, :, :]).then_inc(t.s_sel, 1)
            dve.wait_ge(t.s_gexp, TT)
            step.link(dve.tensor_tensor(t.gate[:, :, :], t.gexp[:, :, :], t.sel[:, :, :], ALU.mult))
            step.link(dve.tensor_reduce(t.room[:, :], t.gate[:, :, :], AX.X, ALU.add))
            step.link(dve.reciprocal(t.room[:, :], t.room[:, :]))
            dve.tensor_tensor(t.gate[:, :, :], t.gate[:, :, :], t.room[:, :].unsqueeze(2).to_broadcast([P, TT, E]), ALU.mult).then_inc(t.s_gate, 1)
            dve.wait_ge(t.s_route, 4)
            step.link(dve.tensor_scalar(t.tie[:, :, :], t.sel[:, :, :], -UNROUTED, UNROUTED, ALU.mult, ALU.add))
            step.add(dve.tensor_tensor(t.place[:, :, :], halves(bank[6][:, 0:TT * E], E), t.tie[:, :, :], ALU.add))
            step.link(dve.tensor_copy(t.cnt[:, :], bank[7][:, 0:E]))
            step.link(dve.tensor_scalar(t.more[:, :], t.cnt[:, :], float(CAP), None, ALU.is_gt))
            for m in range(2, -(-SEQ // CAP)):
                step.link(dve.scalar_tensor_tensor(t.more[:, :], t.cnt[:, :], float(CAP * m), t.more[:, :], ALU.is_gt, ALU.add))
            step.link(dve.tensor_tensor_scan(t.run[:, :], t.kf[:, K_ONE:K_ONE + E], t.more[:, :], 0.0, ALU.mult, ALU.add))
            extra, own, before, isx = (t.tmp[:, c:c + 1] for c in range(4))
            pnum = t.kf[:, K_P:K_P + 1]
            step.link(dve.tensor_scalar(extra, pnum, float(E), None, ALU.subtract))
            step.add(dve.tensor_scalar(isx, pnum, float(E), None, ALU.is_ge))
            step.link(dve.tensor_scalar(t.below[:, :], t.run[:, :], extra, None, ALU.is_le))
            step.link(dve.tensor_reduce(own, t.below[:, :], AX.X, ALU.add))
            step.link(dve.tensor_tensor(t.below[:, :], t.below[:, :], t.more[:, :], ALU.mult))
            step.link(dve.tensor_reduce(before, t.below[:, :], AX.X, ALU.add))
            step.link(dve.tensor_scalar(own, own, float(E - 1), pnum, ALU.min, ALU.subtract))
            step.link(dve.tensor_tensor(own, own, isx, ALU.mult))
            step.add(dve.tensor_scalar(t.listcol[:, 0:1], own, pnum, None, ALU.add))
            step.link(dve.tensor_tensor(extra, extra, before, ALU.subtract))
            step.link(dve.tensor_scalar(extra, extra, 1.0, float(CAP), ALU.add, ALU.mult))
            step.link(dve.tensor_tensor(extra, extra, isx, ALU.mult))
            step.add(dve.tensor_scalar(t.listcol[:, 1:2], t.run[:, E - 1:E], float(E), None, ALU.add))
            step.link(dve.tensor_scalar(own, own, pnum, None, ALU.add))
            step.link(dve.tensor_scalar(t.below[:, :], t.kf[:, K_E:K_E + E], own, None, ALU.is_equal))
            step.link(dve.tensor_tensor(t.below[:, :], t.below[:, :], t.cnt[:, :], ALU.mult))
            step.link(dve.tensor_reduce(own, t.below[:, :], AX.X, ALU.add))
            step.link(dve.tensor_tensor(own, own, extra, ALU.subtract))
            step.link(dve.tensor_scalar(t.listcol[:, 2:3], own, 0.0, None, ALU.max))
            dve.sem_inc(t.s_list, 1)
            dve.tensor_scalar(t.diag[:, :], ident, extra, None, ALU.mult).then_inc(t.s_diag, 1)
            for j in range(TT):
                step.add(dve.tensor_copy(t.bring[:, j, :, 0:3], t.kb[:, B_TOK + 3 * j:B_TOK + 3 * j + 3].unsqueeze(1).to_broadcast([P, E, 3])))
            dve.wait_ge(t.s_gate, 1)
            dve.wait_ge(t.s_route, 5)
            step.add(dve.tensor_copy(t.gT[:, :], bank[5][:, P:2 * P]))
            step.link(dve.tensor_copy(t.bring[:, :, :, 3], t.gate[:, :, :]))
            dve.sem_inc(t.s_gT, 1)
            step.link(dve.tensor_tensor(t.gate[:, :, :], t.gate[:, :, :], t.bring[:, :, :, 3], ALU.subtract))
            step.link(dve.tensor_copy(t.bring[:, :, :, 4], t.gate[:, :, :]))
            step.link(dve.tensor_tensor(t.gate[:, :, :], t.gate[:, :, :], t.bring[:, :, :, 4], ALU.subtract))
            step.link(dve.tensor_copy(t.bring[:, :, :, 5], t.gate[:, :, :]))
            for j in range(TT):
                for c in range(2):
                    dve.wait_ge(t.s_bias, 2 * j + c + 1)
                    dve.tensor_tensor(t.h[:, j, c * SEQ:(c + 1) * SEQ], t.h[:, j, c * SEQ:(c + 1) * SEQ], bank[2 * (j % 2) + c][:, :], ALU.add).then_inc(t.s_acc, 1)
            dve.wait_ge(t.s_first, 1)
            dve.tensor_copy(t.first[:, :], bank[4][:, 0:P]).then_inc(t.s_efirst, 1)


def mixture(nc, t):
    bank = t.bank
    ident = t.kf[:, K_ID:K_ID + P]
    PT, PX, PY = (5, 0, 1), (3, 4), (6, 7)

    with nc.Block() as block:

        def expert_of(eng, i):
            return eng.value_load(t.lists[0:1, bass.ds(i * LIST, 1)], min_val=0, max_val=E - 1)

        def block_count(eng):
            return eng.value_load(t.lists[0:1, 1:2], min_val=E, max_val=E + MORE)

        @block.sync
        def _(sp):
            n = block_count(sp)
            with sp.Fori(0, n - 1) as i:
                e = expert_of(sp, i + 1)
                for k in range(KB):
                    sp.wait_ge(t.s_w1used, i * KB + k + 1)
                    sp.dma_start(t.w1[:, k, :], t.d_w1[bass.ds(e, 1), k * P:(k + 1) * P, :].rearrange("a p n -> (a p) n")).then_inc(t.s_w1[k], 16)
                for j in range(4):
                    sp.wait_ge(t.s_w2used, i * 4 + j + 1)
                    sp.dma_start(t.w2[:, j, :, :], t.d_w2[bass.ds(e, 1), j * FC:(j + 1) * FC, :].rearrange("e (a p) n -> p (e a) n", p=P)).then_inc(t.s_w2[j], 16)

        @block.gpsimd
        def _(pool):
            n = block_count(pool)

            def gather():
                pool.indirect_dma_start(out=t.xg[:, :], out_offset=None, in_=t.d_u2, in_offset=bass.IndirectOffsetOnAxis(ap=t.gidx[:, 0:1], axis=0)).then_inc(t.s_gather, 16)

            pool.wait_ge(t.s_gidx, 1)
            gather()
            with pool.Fori(0, n) as i:
                pool.wait_ge(t.s_gidx, i + 2)
                pool.wait_ge(t.s_xt, i * 2 + 2)
                pool.sem_inc(t.s_go, 1)
                gather()
                for g in range(NG):
                    pool.wait_ge(t.s_ysb, i * NG + g + 2)
                    pool.wait_ge(t.s_sidx, i + 1)
                    pool.sem_inc(t.s_go, 1)
                    pool.indirect_dma_start(out=t.d_acc4, out_offset=bass.IndirectOffsetOnAxis(ap=t.sidx[:, g:g + 1], axis=0), in_=t.ysb[:, g, :],
                                            in_offset=None, compute_op=ALU.add).then_inc(t.s_scat, 16)
            pool.wait_ge(t.s_gather, n * 16 + 16)
            pool.wait_ge(t.s_scat, n * 48 + 48)

        @block.scalar
        def _(act):
            n = block_count(act)

            def turn(i):
                act.wait_ge(t.s_xt, i * 2 + 1)
                act.activation(t.xe[:, 0:4, :], halves(bank[PX[0]][:, 0:4 * CAP], CAP), ACT.Copy).then_inc(t.s_xe, 1)

            act.dma_start(t.b1[:, :], t.d_b1[0]).then_inc(t.s_b1, 16)
            turn(0)
            with act.Fori(0, n) as i:
                for g in range(NG):
                    act.wait_ge(t.s_glu, i * NG + g + 1)
                    act.activation(t.sig[:, g, :], t.hb[:, g, 0:FC], ACT.Sigmoid, scale=ALPHA).then_inc(t.s_sig, 1)
                e = expert_of(act, i + 1)
                act.dma_start(t.b1[:, :], t.d_b1[bass.ds(e, 1)].rearrange("a p n -> (a p) n")).then_inc(t.s_b1, 16)
                turn(i + 1)
                act.wait_ge(t.s_scat, i * 48 + 48)
                for g in range(NG):
                    if g < NG - 1:
                        act.wait_ge(t.s_y, i * (NG - 1) + g + 1)
                    else:
                        act.wait_ge(t.s_w2used, i * 4 + 4)
                    act.activation(t.ysb[:, g, :], bank[PY[g % 2]][:, 0:FC], ACT.Copy, scale=t.sgate[:, bass.ds(i * NG + g, 1)]).then_inc(t.s_ysb, 1)
            act.wait_ge(t.s_b1, n * 16 + 16)
            act.sem_inc(t.s_go, 1)

        @block.tensor
        def _(pe):
            n = block_count(pe)

            def dispatch(i):
                e = expert_of(pe, i)
                pe.wait_ge(t.s_hot, i + 1)
                for g in range(NG):
                    for j in range(TT):
                        pe.matmul(bank[5][:, 8 * g:8 * g + 6], t.hot[:, j, g * P:(g + 1) * P], t.bring[:, j, bass.ds(e, 1), :].rearrange("p a n -> p (a n)"),
                                  start=(j == 0), stop=(j == TT - 1))
                for j in range(TT):
                    mm = pe.matmul(bank[5][0:CAP, 32:35], t.hot[:, j, NG * P:], t.bring[:, j, bass.ds(e, 1), 0:3].rearrange("p a n -> p (a n)"),
                                   start=(j == 0), stop=(j == TT - 1), tile_position=(0, 0))
                mm.then_inc(t.s_disp, 1)

            def turn(i):
                pe.wait_ge(t.s_gather, i * 16 + 16)
                for c in range(2):
                    for x in range(4):
                        k = 4 * c + x
                        mm = pe.transpose(bank[PX[c]][:, x * CAP:(x + 1) * CAP], t.xg[:, k * P:(k + 1) * P], ident[0:CAP, 0:CAP])
                    mm.then_inc(t.s_xt, 1)

            def up(k, g):
                for c in range(4):
                    cols = t.w1[:, k, :].rearrange("p (a n) -> p a n", a=2)[:, :, c * FC:(c + 1) * FC]
                    mm = pe.matmul(halves(bank[g][c * G:(c + 1) * G, :], FC), t.xe[:, k, g * G:(g + 1) * G], cols,
                                   start=(k == 0), stop=(k == KB - 1), tile_position=(0, c * G))
                return mm

            def turn_act(i, g):
                pe.wait_ge(t.s_a, i * NG + g + 1)
                for x in range(2):
                    mm = pe.transpose(bank[PT[g]][:, x * P:(x + 1) * P], t.a[:, g, x * P:(x + 1) * P], ident)
                mm.then_inc(t.s_at, 1)

            def down(i, g, last):
                pe.wait_ge(t.s_ae, i * NG + g + 2)
                pe.wait_ge(t.s_ysb, i * NG + (2 if g == 2 else 1))
                for b in range(4):
                    if g == 0:
                        pe.wait_ge(t.s_w2[b], i * 16 + 16)
                    for x in range(2):
                        for c in range(4):
                            mm = pe.matmul(bank[PY[g % 2]][c * G:(c + 1) * G, 0:FC], t.aT[:, g, x, b * G:(b + 1) * G], t.w2[:, b, x, c * FC:(c + 1) * FC],
                                           start=(b == 0 and x == 0), stop=(b == 3 and x == 1), tile_position=(0, c * G))
                    if g == last:
                        mm.then_inc(t.s_w2used, 1)
                if g < last:
                    mm.then_inc(t.s_y, 1)

            def work(i, groups):
                last = groups - 1
                for k in range(4):
                    pe.wait_ge(t.s_w1[k], i * 16 + 16)
                    for g in range(groups):
                        mm = up(k, g)
                    mm.then_inc(t.s_w1used, 1)
                    if k == 0:
                        pe.wait_ge(t.s_slots, i + 1)
                        dispatch(i + 1)
                for g in range(groups):
                    for k in range(4, KB):
                        if g == 0:
                            pe.wait_ge(t.s_w1[k], i * 16 + 16)
                        mm = up(k, g)
                        if g == last:
                            mm.then_inc(t.s_w1used, 1)
                    if g < last:
                        mm.then_inc(t.s_up, 1)
                if groups < NG:
                    pe.wait_ge(t.s_w1used, i * KB + KB)
                    pe.sem_inc(t.s_up, 1)
                pe.wait_ge(t.s_slots, i + 2)
                turn_act(i, 0)
                turn(i + 1)
                turn_act(i, 1)
                down(i, 0, last)
                if groups == NG:
                    turn_act(i, 2)
                else:
                    pe.wait_ge(t.s_ae, i * NG + 3)
                    pe.sem_inc(t.s_at, 1)
                down(i, 1, last)
                if groups == NG:
                    down(i, 2, last)
                else:
                    pe.wait_ge(t.s_w2used, i * 4 + 4)
                    pe.sem_inc(t.s_y, 1)

            dispatch(0)
            turn(0)
            with pe.Fori(0, n) as i:
                pe.wait_ge(t.s_xe, i * 2 + 2)
                pe.wait_ge(t.s_hfree, i * NG + NG)
                pe.wait_ge(t.s_ae, i * NG + 1)
                tokens = pe.value_load(t.lists[0:1, bass.ds(i * LIST + 2, 1)], min_val=0, max_val=SEQ)
                with pe.If(tokens > (NG - 1) * G):
                    work(i, NG)
                with pe.Else():
                    work(i, NG - 1)

        @block.vector
        def _(dve):
            n = block_count(dve)
            dve.sem_inc(t.s_hfree, NG)
            dve.sem_inc(t.s_ysb, 1)
            dve.sem_inc(t.s_ae, 1)

            def find(i, chain, base):
                e = expert_of(dve, i)
                for j in range(TT):
                    ins = dve.tensor_scalar(t.hot[:, j, :], t.kb[:, B_SLOT:B_SLOT + HOT], t.first[:, bass.ds(i, 1)],
                                            t.place[:, j, bass.ds(e, 1)], ALU.add, ALU.is_equal)
                    if j < TT - 1:
                        chain.add(ins)
                chain.sync(0, base)
                ins.then_inc(t.s_hot, 1)

            def slots(i, chain, base):
                dve.wait_ge(t.s_disp, i + 1)
                chain.add(dve.tensor_copy(t.slot[:, :, :], bank[5][:, 0:24].rearrange("p (a n) -> p a n", n=8)[:, :, 0:6]))
                dve.tensor_copy(t.rowf[:, 0:2], bank[5][0:CAP, 32:34]).then_inc(t.s_slots, 1)
                chain.sync(0, base)
                dve.wait_ge(t.s_slots, i + 2)
                q, r, one = (t.slot[:, :, c] for c in range(3))
                chain.add(dve.tensor_tensor(t.rowf[:, 2:3], t.rowf[:, 0:1], t.rowf[:, 1:2], ALU.add))
                chain.add(dve.tensor_tensor(q, q, r, ALU.add))
                chain.link(dve.tensor_tensor(one, one, t.kf[:, K_PAD:K_PAD + NG], ALU.mult), base)
                dve.tensor_scalar(t.gidx[:, :], t.rowf[:, 2:3], 0.25, None, ALU.mult).then_inc(t.s_gidx, 1)
                chain.add(dve.tensor_tensor(q, q, t.kf[:, K_ROW:K_ROW + NG], ALU.add))
                chain.link(dve.tensor_tensor(t.slot[:, :, 3], t.slot[:, :, 3], t.slot[:, :, 4], ALU.add), base)
                chain.link(dve.tensor_tensor(t.srow[:, bass.ds(i * NG, NG)], q, one, ALU.add), base)
                chain.link(dve.tensor_tensor(t.sgate[:, bass.ds(i * NG, NG)], t.slot[:, :, 3], t.slot[:, :, 5], ALU.add), base)

            def turn(i):
                dve.wait_ge(t.s_xt, i * 2 + 2)
                dve.tensor_copy(t.xe[:, 4:8, :], halves(bank[PX[1]][:, 0:4 * CAP], CAP)).then_inc(t.s_xe, 1)

            def gated(i, g, chain, base):
                if g < NG - 1:
                    dve.wait_ge(t.s_up, i * (NG - 1) + g + 1)
                else:
                    dve.wait_ge(t.s_w1used, i * KB + KB)
                if g == 0:
                    dve.wait_ge(t.s_b1, i * 16 + 16)
                dve.tensor_tensor(t.hb[:, g, :], bank[g][:, :], t.b1[:, :], ALU.add).then_inc(t.s_hfree, 1)
                dve.wait_ge(t.s_hfree, i * NG + g + 1 + NG)
                dve.tensor_scalar(t.hb[:, g, 0:FC], t.hb[:, g, 0:FC], LIMIT, None, ALU.min).then_inc(t.s_glu, 1)
                chain.link(dve.tensor_scalar(t.hb[:, g, FC:], t.hb[:, g, FC:], LIMIT, -LIMIT, ALU.min, ALU.max), base)
                dve.wait_ge(t.s_glu, i * NG + g + 1)
                chain.link(dve.scalar_tensor_tensor(t.a[:, g, :], t.hb[:, g, FC:], 1.0, t.hb[:, g, 0:FC], ALU.add, ALU.mult), base)

            def swiglu(i, g):
                dve.wait_ge(t.s_sig, i * NG + g + 1)
                dve.tensor_tensor(t.a[:, g, :], t.a[:, g, :], t.sig[:, g, :], ALU.mult).then_inc(t.s_a, 1)

            def turned(i, g):
                dve.wait_ge(t.s_at, i * NG + g + 1)
                dve.tensor_copy(t.aT[:, g, :, :], halves(bank[PT[g]][:, 0:2 * P], P)).then_inc(t.s_ae, 1)

            pre = Chain(dve, t.s_pre)
            dve.sem_inc(t.s_slots, 1)
            find(0, pre, 0)
            slots(0, pre, 0)
            turn(0)
            STEPS = 3 + 8 + 2 * NG
            with dve.Fori(0, n) as i:
                step, base = Chain(dve, t.s_step), i * STEPS
                find(i + 1, step, base)
                slots(i + 1, step, base)
                dve.wait_ge(t.s_scat, i * 48 + 48)
                dve.tensor_copy(t.sidx[:, :], t.srow[:, bass.ds(i * NG, NG)]).then_inc(t.s_sidx, 1)
                for g in range(2):
                    gated(i, g, step, base)
                    swiglu(i, g)
                turned(i, 0)
                gated(i, 2, step, base)
                turn(i + 1)
                turned(i, 1)
                swiglu(i, 2)
                turned(i, 2)
                assert step.n == STEPS, step.n


def finish(nc, t):
    with nc.Block() as block:

        @block.sync
        def _(sp):
            sp.dma_start(t.gfin[:, :], t.d_gfin.partition_broadcast(P)).then_inc(t.s_fin, 16)
            for j in range(TT):
                sp.dma_start(t.h[:, j, :], t.d_acc[j * P:(j + 1) * P, :]).then_inc(t.s_hin[j], 16)
            for j in range(TT):
                sp.wait_ge(t.s_res, j + 1)
                sp.dma_start(t.out[j * P:(j + 1) * P, :], t.u2[:, j, :]).then_inc(t.s_out, 16)
            sp.wait_ge(t.s_out, 16 * TT)

        @block.scalar
        def _(act):
            for j in range(TT):
                act.wait_ge(t.s_hin[j], 16)
                act.activation(t.u2[:, j, :], t.h[:, j, :], ACT.Square, accum_out=t.ss[:, j:j + 1]).then_inc(t.s_fss, 1)
                act.wait_ge(t.s_fss, j + 1)
                act.activation(t.ss[:, j:j + 1], t.ss[:, j:j + 1], ACT.Sqrt, bias=t.eps[:, 0:1], scale=1.0 / D).then_inc(t.s_froot, 1)

        @block.vector
        def _(dve):
            dve.wait_ge(t.s_fin, 16)
            for j in range(TT):
                dve.wait_ge(t.s_froot, j + 1)
                dve.reciprocal(t.ss[:, j:j + 1], t.ss[:, j:j + 1]).then_inc(t.s_frec, 1)
                dve.wait_ge(t.s_frec, j + 1)
                dve.scalar_tensor_tensor(t.u2[:, j, :], t.h[:, j, :], t.ss[:, j:j + 1], t.gfin[:, :], ALU.mult, ALU.mult).then_inc(t.s_res, 1)


def build(nc, io):
    with ExitStack() as ctx:
        t = Tensors()
        t.d_kf = io["d_kf"]
        t.d_kb = io["d_kb"]
        t.d_dense = io["d_dense"]
        t.d_chan = io["d_chan"]
        t.d_x = io["d_x"]
        t.d_xT = io["d_xT"]
        t.d_pos = io["d_pos"]
        t.d_sinks = io["d_sinks"]
        t.d_wr = io["d_wr"]
        t.d_gffn = io["d_gffn"]
        t.d_gfin = io["d_gfin"]
        t.d_b2 = io["d_b2"]
        t.d_b1 = io["d_b1"]
        t.d_w1 = io["d_w1"]
        t.d_w2 = io["d_w2"]
        t.out = io["out"]

        def sb(name, shape, dt=F32):
            return ctx.enter_context(nc.sbuf_tensor(name, shape, dt))

        def rounded(name, shape):
            tensor = sb(name, shape)
            place = nc.sbuf_base - 4 * shape[1]
            return tensor, nc.alloc_sbuf_tensor_at(name + "_r", tuple(shape), F32R, offset=place)

        def sem(name):
            return ctx.enter_context(nc.semaphore(name))

        def sems(name, n):
            return [sem(f"{name}_{i}") for i in range(n)]

        t.d_acc = nc.dram_tensor("acc", (SEQ + P, D), F32, kind="Internal").ap()
        t.d_acc4 = t.d_acc.rearrange("r (c n) -> (r c) n", n=FC)
        t.d_u2 = nc.dram_tensor("u2_rows", (SEQ, D), F32, kind="Internal").ap()
        t.d_list = nc.dram_tensor("block_list", (P, LIST), I32, kind="Internal").ap()

        big, big_r = rounded("big", [P, 24576])
        t.w1 = big[:, 0:16384].rearrange("p (k n) -> p k n", k=KB)
        t.w2 = big[:, 16384:24576].rearrange("p (j a n) -> p j a n", j=4, a=2)
        t.qT = halves(big[:, 0:4096], SEQ)
        t.gates = halves(big[:, 4096:12288], SEQ)
        t.cT = halves(big[:, 12288:12288 + KB * CW], CW)
        t.cv = halves(big[:, 16640:20736], SEQ)
        t.kT = halves(big[:, 20736:22016], SEQ + WIN)
        t.v = halves(big[:, 22016:22656], P)
        t.vT = big[:, 22656:23168]
        t.cv_hi = t.mix_hi = halves(big_r[:, 12288:16384], SEQ)
        t.cv_lo = halves(big_r[:, 16640:20736], SEQ)
        xT, xT_r = rounded("xT", [P, 4096])
        t.xT = halves(xT[:, :], SEQ)
        t.u2 = halves(xT[:, :], D)
        t.o_lo = halves(xT_r[:, :], SEQ)
        uT, uT_r = rounded("uT", [P, 4096])
        t.uT = halves(uT[:, :], SEQ)
        t.h = halves(uT[:, :], D)
        t.o_hi = t.u_lo = halves(uT_r[:, :], SEQ)
        ring, ring_r = rounded("ring", [P, 4096])
        t.wring, t.wlo = halves(ring[:, :], D), halves(ring_r[:, :], D)
        t.xg = ring[0:CAP, 0:1024]
        t.xe = halves(ring[:, 1024:1792], CAP)
        t.hb = halves(ring[:, 1792:3328], 2 * FC)
        t.sig = halves(ring[:, 3328:4096], FC)
        t.gfin = ring[:, 0:1024]
        mix, mix_r = rounded("mix", [P, 4096])
        t.mix = t.u2T = halves(mix[:, :], SEQ)
        t.u_hi = t.mix_lo = halves(mix_r[:, :], SEQ)
        t.a = halves(mix[:, 0:768], FC)
        t.aT = mix[:, 768:1536].rearrange("p (g x n) -> p g x n", g=NG, x=2)
        t.ysb = halves(mix[:, 1536:2304], FC)
        t.hot = halves(mix[:, 2304:2304 + TT * HOT // 2].bitcast(BF16), HOT)
        sm, sm_r = rounded("sm", [P, 2048])
        t.sm = sm[:, :].rearrange("p (u x n) -> p u x n", u=2, x=4)
        t.gffn, t.b2 = sm[:, 0:1024], sm[:, 1024:2048]
        t.hi_early = (sm_r[:, 0:1024], sm_r[:, 1024:2048])
        t.pT = sb("pT", [P, 2, 4, P])
        rope, rope_r = rounded("rope", [P, 1024])
        t.sin, t.cos, t.junk, t.kb32 = rope[:, 0:512], rope[:, 512:1024], rope[:, :], rope[:, 0:B_W]
        angles, angles_r = rounded("angles", [P, 1024])
        t.ang, t.pos_i, t.zrow = angles[:, 0:512], angles[:, 512:1024].bitcast(I32), angles[:, :]
        t.hi_late = (rope_r[:, :], angles_r[:, :])
        t.rstd, t.odd, t.b1 = (sb(x, [P, 512]) for x in ("rstd", "odd", "b1"))
        t.kf, t.kb, t.chan = sb("kf", [P, K_W]), sb("kb", [P, B_W], BF16), sb("chan", [P, V_W])
        t.sinks, t.wr, t.eps = sb("sinks_sb", [P, HEADS]), sb("wr", [P, KB * E]), sb("eps", [P, 1])
        t.negm, t.rsum, t.esink, t.mx = (sb(x, [P, NU, 4]) for x in ("negm", "rsum", "esink", "mx"))
        t.ss, t.nv1, t.room = (sb(x, [P, TT]) for x in ("ss", "nv1", "room"))
        t.lT, t.gT, t.diag, t.first = (sb(x, [P, P]) for x in ("lT", "gT", "diag", "first"))
        t.logits, t.sel, t.tie, t.rank, t.gexp, t.gate, t.place = (
            sb(x, [P, TT, E]) for x in ("logits", "sel", "tie", "rank", "gexp", "gate", "place"))
        t.selb, t.top = sb("selb", [P, TT, E], BF16), sb("top", [P, TT, 8])
        t.cnt, t.more, t.run, t.below = (sb(x, [P, E]) for x in ("cnt", "more", "run", "below"))
        t.tmp, t.listcol, t.lists = sb("tmp", [P, 4]), sb("listcol", [P, LIST], I32), sb("lists", [1, LIST * P], I32)
        t.bring = sb("bring", [P, TT, E, 6], BF16)
        t.slot, t.rowf, t.gidx, t.sidx = sb("slot", [P, NG, 6]), sb("rowf", [CAP, 3]), sb("gidx", [CAP, 1], I32), sb("sidx", [P, NG], I32)
        t.srow, t.sgate = sb("srow", [P, NG * 64]), sb("sgate", [P, NG * 64])
        t.bank = [ctx.enter_context(nc.psum_tensor(f"bank{i}", [P, 512], F32)) for i in range(8)]

        t.s_const = sem("s_const")
        t.s_sq = sem("s_sq")
        t.s_sqodd = sem("s_sqodd")
        t.s_lnsq = sem("s_lnsq")
        t.s_whi = sem("s_whi")
        t.s_wlo = sem("s_wlo")
        t.s_hi = sem("s_hi")
        t.s_lo = sem("s_lo")
        t.s_olo = sem("s_olo")
        t.s_vt = sem("s_vt")
        t.s_v = sem("s_v")
        t.s_stat = sem("s_stat")
        t.s_eps = sem("s_eps")
        t.s_root = sem("s_root")
        t.s_ang = sem("s_ang")
        t.s_rope = sem("s_rope")
        t.s_prod = sem("s_prod")
        t.s_evac = sem("s_evac")
        t.s_gated = sem("s_gated")
        t.s_cent = sem("s_cent")
        t.s_lnt = sem("s_lnt")
        t.s_lns = sem("s_lns")
        t.s_ln = sem("s_ln")
        t.s_max = sem("s_max")
        t.s_exp = sem("s_exp")
        t.s_pt = sem("s_pt")
        t.s_pv = sem("s_pv")
        t.s_ept0 = sem("s_ept0")
        t.s_ept1 = sem("s_ept1")
        t.s_eo = sem("s_eo")
        t.s_late = sem("s_late")
        t.s_h = sem("s_h")
        t.s_ss = sem("s_ss")
        t.s_ut = sem("s_ut")
        t.s_eut0 = sem("s_eut0")
        t.s_eut1 = sem("s_eut1")
        t.s_top = sem("s_top")
        t.s_gexp = sem("s_gexp")
        t.s_uT = sem("s_uT")
        t.s_rot = sem("s_rot")
        t.s_swap = sem("s_swap")
        t.s_conv = sem("s_conv")
        t.s_masked = sem("s_masked")
        t.s_score = sem("s_score")
        t.s_prob = sem("s_prob")
        t.s_merge = sem("s_merge")
        t.s_u2 = sem("s_u2")
        t.s_route = sem("s_route")
        t.s_lt = sem("s_lt")
        t.s_sel = sem("s_sel")
        t.s_gate = sem("s_gate")
        t.s_gT = sem("s_gT")
        t.s_acc = sem("s_acc")
        t.s_bias = sem("s_bias")
        t.s_diag = sem("s_diag")
        t.s_first = sem("s_first")
        t.s_efirst = sem("s_efirst")
        t.s_dve = sem("s_dve")
        t.s_tap = sem("s_tap")
        t.s_zero = sem("s_zero")
        t.s_scat = sem("s_scat")
        t.s_x = sem("s_x")
        t.s_u2out = sem("s_u2out")
        t.s_list = sem("s_list")
        t.s_listout = sem("s_listout")
        t.s_listin = sem("s_listin")
        t.s_accout = sem("s_accout")
        t.s_w1used = sem("s_w1used")
        t.s_w2used = sem("s_w2used")
        t.s_gather = sem("s_gather")
        t.s_gidx = sem("s_gidx")
        t.s_xt = sem("s_xt")
        t.s_ysb = sem("s_ysb")
        t.s_sidx = sem("s_sidx")
        t.s_xe = sem("s_xe")
        t.s_b1 = sem("s_b1")
        t.s_glu = sem("s_glu")
        t.s_sig = sem("s_sig")
        t.s_y = sem("s_y")
        t.s_hot = sem("s_hot")
        t.s_disp = sem("s_disp")
        t.s_a = sem("s_a")
        t.s_at = sem("s_at")
        t.s_ae = sem("s_ae")
        t.s_hfree = sem("s_hfree")
        t.s_up = sem("s_up")
        t.s_slots = sem("s_slots")
        t.s_pre = sem("s_pre")
        t.s_step = sem("s_step")
        t.s_go = sem("s_go")
        t.s_fin = sem("s_fin")
        t.s_res = sem("s_res")
        t.s_out = sem("s_out")
        t.s_fss = sem("s_fss")
        t.s_froot = sem("s_froot")
        t.s_frec = sem("s_frec")
        t.s_xT = sems("s_xT", 4)
        t.s_w = sems("s_w", NSLOT)
        t.s_w1 = sems("s_w1", KB)
        t.s_w2 = sems("s_w2", 4)
        t.s_hin = sems("s_hin", TT)

        dense_half(nc, t)
        mixture(nc, t)
        finish(nc, t)


def constants():
    p = np.arange(P)
    kf = np.zeros((P, K_W), np.float32)
    kf[:, K_ID:K_ID + P] = np.eye(P)
    kf[:, K_MEAN:K_MEAN + P] = 1.0 / D
    kf[:, K_ONE:K_ONE + P] = 1.0
    rot = HD // 8
    for head in range(2):
        for d in range(rot):
            kf[head * HD + d + rot, K_ROT + head * HD + d] = -1.0
            kf[head * HD + d, K_ROT + head * HD + d + rot] = 1.0
            freq = np.float32(500000.0) ** np.float32(-2.0 * d / (2 * rot))
            kf[head * HD + d, K_FREQ] = kf[head * HD + d + rot, K_FREQ] = freq
    q, k = np.arange(WIN)[:, None] + WIN, np.arange(2 * WIN)[None, :]
    band = (q - k >= 0) & (q - k < WIN)
    kf[:, K_MASK:K_MASK + 256] = np.where(band, 0.0, MASKED)
    kf[:, K_MASK + 256:K_MASK + 512] = np.where(band & (k >= WIN), 0.0, MASKED)
    kf[:, K_HALFPI] = np.pi / 2
    tile, token = p // G, p % G
    for g in range(NG):
        pad = 4 * (SEQ + g * G + token)
        kf[:, K_PAD + g] = -pad
        kf[:, K_ROW + g] = pad + tile
    kf[:, K_P] = p
    kf[:, K_E:K_E + E] = np.arange(E)
    kb = np.zeros((P, B_W), np.float32)
    kb[:, B_TRI:B_TRI + P] = p[:, None] < p[None, :]
    kb[:, B_ONE:B_ONE + P] = 1.0
    for g in range(NG):
        kb[:, B_SLOT + g * P:B_SLOT + (g + 1) * P] = g * G + token[None, :]
    kb[:, B_SLOT + NG * P:B_SLOT + HOT] = np.arange(CAP)
    for j in range(TT):
        kb[:, B_TOK + 3 * j:B_TOK + 3 * j + 3] = np.stack([np.full(P, 4 * P * j), 4 * p, np.ones(P)], 1)
    return kf, kb


def lay_out(a):
    def blocks(w):
        n = w.shape[1] // P
        return w.reshape(KB, P, n, P).transpose(2, 1, 0, 3).reshape(n, P, KB * P)

    def by_channel(v):
        return v.reshape(KB, P).T

    w_in = a["w_in"][0]
    conv_value, conv_gate, wq, wk, wv, gates = np.split(w_in, np.cumsum([D, D, D, KV * HD, KV * HD]), axis=1)
    pairs = np.stack([blocks(conv_value), blocks(conv_gate)], 1).reshape(16, P, D)
    twice = np.concatenate([wk[:, 0:HD], wk[:, 0:HD], wk[:, HD:], wk[:, HD:]], 1)
    dense = np.concatenate([
        pairs, blocks(wq), blocks(twice), blocks(wv), np.zeros((1, P, D), np.float32), blocks(gates),
        blocks(a["w_conv_out"][0]), blocks(a["w_attn_out"][0]), a["w_out"][0].reshape(KB, P, D)])
    kf, kb = constants()
    w_dw = a["w_dw"][0].reshape(TAPS, KB, P).transpose(2, 1, 0).reshape(P, KB * TAPS)
    router_bias = np.tile(a["b_router"][0], TT).reshape(P, 1)
    chan = np.concatenate([w_dw] + [by_channel(a[x][0]) for x in ("b_dw", "g_conv_ln", "b_conv_ln", "g_mix_norm")] + [router_bias], 1)
    sinks = a["attn_sinks"][0].reshape(4, 2, 2).transpose(0, 2, 1).reshape(HEADS)
    b1 = a["b_mlp1"][0].reshape(E, 2, 4, FC).transpose(0, 2, 1, 3).reshape(E, 4, 1, 2 * FC)
    return {
        "d_kf": kf, "d_kb": kb, "d_dense": dense, "d_chan": chan,
        "d_x": a["x"][0], "d_xT": a["x"][0].T.reshape(KB, P, SEQ).transpose(1, 0, 2),
        "d_pos": a["positions"].astype(np.int32).reshape(SEQ), "d_sinks": sinks,
        "d_wr": a["w_router"][0].reshape(KB, P, E).transpose(1, 0, 2).reshape(P, KB * E),
        "d_gffn": a["g_ffn_norm"][0], "d_gfin": a["g_final"],
        "d_b2": np.tile(a["b_mlp2"][0], (TT, 1)), "d_b1": np.broadcast_to(b1, (E, 4, G, 2 * FC)).reshape(E, P, 2 * FC),
        "d_w1": a["w_mlp1"][0], "d_w2": a["w_mlp2"][0],
    }


def kernel(**inputs):
    import concourse.bacc as bacc
    from concourse.bass_utils import run_bass_kernel_spmd as run

    arrays = {k: np.ascontiguousarray(v) for k, v in lay_out({k: np.asarray(v) for k, v in inputs.items()}).items()}
    nc = bacc.Bacc("TRN2", target_bir_lowering=False, num_devices=1)
    io = {name: nc.dram_tensor(f"in_{name}", x.shape, mybir.dt.from_np(x.dtype), kind="ExternalInput").ap() for name, x in arrays.items()}
    io["out"] = nc.dram_tensor("out_rows", (SEQ, D), F32, kind="ExternalOutput").ap()
    build(nc, io)
    r = run(nc, [{f"in_{k}": v for k, v in arrays.items()}], core_ids=[0])
    return r.results[0]["out_rows"].reshape(1, SEQ, D)
```

```python
from contextlib import ExitStack

import numpy as np

import concourse.bass as bass
from concourse import mybir

F32 = mybir.dt.float32
F32R = mybir.dt.float32r
BF16 = mybir.dt.bfloat16
I32 = mybir.dt.int32
ALU = mybir.AluOpType
ACT = mybir.ActivationFunctionType
AX = mybir.AxisListType

P = 128
D = 1024
SEQ = 512
TT = SEQ // P
KB = D // P
TAPS = 31
HALO = TAPS - 1
CW = SEQ + HALO
HEADS = 16
KV = 2
HD = 64
WIN = 128
SCALE = HD ** -0.5
EPS = 1e-5
E = 32
TOPK = 4
CAP = 96
G = 32
NG = CAP // G
K_EACH = 5
FC = 256
LIMIT = 7.0
ALPHA = 1.702
MORE = (SEQ * TOPK) // CAP
NSLOT = 4
LIST = 3
I_MEAN, I_VAR = 10, 13
NU = 16

C_CONV, C_Q, C_KV, C_GATE, C_COUT, C_AOUT, C_WOUT, N_CHUNK = 0, 16, 24, 28, 44, 52, 60, 68
SKIP = 27


def used(n):
    return n + 1 if isinstance(n, int) and n < SKIP else n


def loads(n):
    return n // NSLOT + 1 - (n > SKIP and n % NSLOT == SKIP % NSLOT)


def upper(t, n):
    return (t.hi_early if n < C_COUT else t.hi_late)[(used(n) - 1) % 2]


K_ID, K_MEAN, K_ONE, K_ROT, K_MASK = 0, 128, 256, 384, 512
K_FREQ = K_MASK + 512
K_HALFPI = K_FREQ + 1
K_PAD = K_HALFPI + 1
K_ROW = K_PAD + NG
K_P = K_ROW + NG
K_E = K_P + 1
K_TILE = K_E + E
K_W = K_TILE + TT
B_TRI, B_ONE, B_SLOT = 0, 128, 256
HOT = NG * P + CAP
B_TOK = B_SLOT + HOT
B_W = B_TOK + TT * 3
V_DW, V_BDW, V_GLN, V_BLN, V_GMIX, V_BR = 0, 248, 256, 264, 272, 280
V_W = 281

TWO_PI = 2.0 * np.pi
PI_A = 6.28125
PI_B = float(np.floor((TWO_PI - PI_A) * 2**20) / 2**20)
PI_C = float(TWO_PI - PI_A - PI_B)
ROUND = 1.5 * 2.0**23
MASKED = -1e30
CONV_SUM = (C_KV, C_KV + 1, C_KV + 2, C_GATE + 2, C_GATE + 5, C_GATE + 9, C_GATE + I_MEAN + 1)
UNROUTED = 4096.0
NOWHERE = 1024.0


class Tensors:
    pass


class Chain:

    def __init__(self, eng, sem):
        self.eng, self.sem, self.n = eng, sem, 0

    def add(self, ins):
        ins.then_inc(self.sem, 1)
        self.n += 1

    def sync(self, back=0, base=0):
        self.eng.wait_ge(self.sem, base + self.n - back)

    def link(self, ins, base=0):
        self.add(ins)
        self.sync(0, base)


def at(ap3, i):
    return ap3[:, bass.ds(i, 1), :].rearrange("p a n -> p (a n)")


def halves(ap, n):
    return ap.rearrange("p (a n) -> p a n", n=n)


def rotated(t, j):
    return t.kT[:, j, WIN:] if j < KV else t.qT[:, j - KV, :]


def bias_part(x):
    return x % TT, x // TT, (0, 1, 2, 3, 6, 7, 0, 1)[x]


def gated_bias(pe, t, x):
    j, c, b = bias_part(x)
    pe.matmul(t.bank[b][:, :], t.gT[:, j, :], t.b2[:, c * SEQ:(c + 1) * SEQ], start=True, stop=True).then_inc(t.s_bias, 1)


def heads_of(ap, u):
    hp, blk = (u // 8) * 4 + (u % 2) * 2, (u // 2) % 4
    return ap[:, hp:hp + 2, blk * WIN:(blk + 1) * WIN]


def dense_half(nc, t):
    bank = t.bank
    ident = t.kf[:, K_ID:K_ID + P]
    eps = t.eps[:, 0:1]

    with nc.Block() as block:

        @block.sync
        def _(sp):
            for q in range(4):
                sp.dma_start(t.xT[:, 2 * q:2 * q + 2, :], t.d_xT[:, 2 * q:2 * q + 2, :]).then_inc(t.s_xT[q], 16)
                if q == 0:
                    sp.dma_start(t.kf[:, :], t.d_kf).then_inc(t.s_kf, 16)
            for s in range(NSLOT):
                sp.dma_start(t.wring[:, s, :], t.d_dense[s]).then_inc(t.s_w[s], 16)
            with sp.Fori(1, C_KV // NSLOT) as r:
                for s in range(NSLOT):
                    sp.wait_ge(t.s_prod, (r - 1) * NSLOT + s + 1)
                    sp.dma_start(t.wring[:, s, :], t.d_dense[bass.ds(r * NSLOT + s, 1)].rearrange("a p n -> (a p) n")).then_inc(t.s_w[s], 16)
            for n in range(C_KV, C_GATE + NSLOT):
                if n != SKIP:
                    if n - NSLOT != SKIP:
                        sp.wait_ge(t.s_prod, used(n - NSLOT))
                    sp.dma_start(t.wring[:, n % NSLOT, :], t.d_dense[n]).then_inc(t.s_w[n % NSLOT], 16)
            with sp.Fori(C_GATE // NSLOT + 1, N_CHUNK // NSLOT) as r:
                for s in range(NSLOT):
                    sp.wait_ge(t.s_prod, (r - 1) * NSLOT + s)
                    sp.dma_start(t.wring[:, s, :], t.d_dense[bass.ds(r * NSLOT + s, 1)].rearrange("a p n -> (a p) n")).then_inc(t.s_w[s], 16)
            sp.wait_ge(t.s_prod, used(C_WOUT - 1))
            sp.dma_start(t.h[:, :, :], t.d_x.rearrange("(a p) d -> p a d", p=P)).then_inc(t.s_x, 16)
            sp.wait_ge(t.s_merge, 2 * KB)
            for k in range(KB - 2):
                sp.dma_start(t.w1[:, k, :], t.d_w1[0, k * P:(k + 1) * P, :]).then_inc(t.s_w1[k], 16)
            for j in range(4):
                sp.dma_start(t.w2[:, j, :, :], t.d_w2[0, j * FC:(j + 1) * FC, :].rearrange("(a p) n -> p a n", p=P)).then_inc(t.s_w2[j], 16)
            sp.wait_ge(t.s_prod, used(N_CHUNK - 1))
            for k in range(KB - 2, KB):
                sp.dma_start(t.w1[:, k, :], t.d_w1[0, k * P:(k + 1) * P, :]).then_inc(t.s_w1[k], 16)
            for j in range(TT):
                sp.wait_ge(t.s_u2, j + 1)
                sp.dma_start(t.d_u2[j * P:(j + 1) * P, :], t.u2[:, j, :]).then_inc(t.s_u2out, 16)
            sp.wait_ge(t.s_u2out, 16 * TT)

        @block.gpsimd
        def _(pool):
            pool.memset(t.cT[:, :, 0:HALO], 0.0).then_inc(t.s_zero, 1)
            pool.memset(t.kT[:, :, 0:WIN], 0.0).then_inc(t.s_zero, 1)
            pool.memset(t.v[:, 0, :], 0.0).then_inc(t.s_zero, 1)
            def zero_rows():
                pool.wait_ge(t.s_rope, 2)
                pool.memset(t.zrow[:, :], 0.0).then_inc(t.s_zero, 1)
                pool.wait_ge(t.s_zero, 4)
                pool.dma_start(t.d_acc[SEQ:SEQ + P, :], t.zrow[:, :]).then_inc(t.s_scat, 48)

            def weight_rest(slot, hi, count):
                pool.wait_ge(t.s_whi, count)
                pool.tensor_tensor(t.wlo[:, slot, :], t.wring[:, slot, :], hi.bitcast(F32), ALU.subtract).then_inc(t.s_wlo, 1)

            def rest(x, hi, lo, k, count):
                pool.wait_ge(t.s_hi, count)
                pool.tensor_tensor(lo[:, k, :], x[:, k, :], hi[:, k, :].bitcast(F32), ALU.subtract).then_inc(t.s_lo, 1)

            def add_rows(which, rows, k):
                if k > 1:
                    pool.wait_ge(t.s_csum, which * (KB - 1) + k - 1)
                total = t.csum[:, which, :]
                pool.tensor_tensor(total, rows[:, 0, :] if k == 1 else total, rows[:, k, :], ALU.add).then_inc(t.s_csum, 1)

            def add_conv(k):
                pool.wait_ge(t.s_conv, k + 1)
                add_rows(0, t.cv, k)

            for n in range(2):
                weight_rest(n, upper(t, n), n + 1)
            for k in range(KB):
                rest(t.uT, t.u_hi, t.u_lo, k, k + 1)
            zero_rows()
            for n in range(2, NSLOT):
                weight_rest(n, upper(t, n), n + 1)
            with pool.Fori(1, C_KV // NSLOT) as r:
                for s in range(NSLOT):
                    weight_rest(s, upper(t, s), r * NSLOT + s + 1)
            for n in range(C_KV, C_COUT):
                if n != SKIP:
                    weight_rest(n % NSLOT, upper(t, n), used(n))
                if n in CONV_SUM:
                    add_conv(CONV_SUM.index(n) + 1)
                for k in {I_MEAN + 2: range(1, 4), I_MEAN + 3: range(4, KB)}.get(n - C_GATE, ()):
                    pool.wait_ge(t.s_lnsq, k + 1)
                    add_rows(1, t.xT, k)
                i = n - C_GATE - I_MEAN - 1
                for j in range(2 * i, 2 * i + 2) if 0 <= i < 5 else ():
                    x = rotated(t, j)
                    if j == 0:
                        pool.wait_ge(t.s_evac, C_KV + KV)
                        pool.wait_ge(t.s_scat, 48)
                    if j >= 2:
                        pool.wait_ge(t.s_rot, j - 1)
                    pool.tensor_tensor(t.xcos[:, j % 2, :], x, t.cos[:, :], ALU.mult).then_inc(t.s_xcos, 1)
            for k in range(KB):
                rest(t.cv, t.cv_hi, t.cv_lo, k, KB + k + 1)
            for n in range(C_COUT, C_AOUT + 2):
                weight_rest(n % NSLOT, upper(t, n), used(n))
            for k in range(KB):
                n = C_AOUT + 2 + k
                weight_rest(n % NSLOT, upper(t, n), used(n))
                rest(t.mix, t.mix_hi, t.mix_lo, k, 2 * KB + k + 1)
            for n in range(C_WOUT + 2, N_CHUNK):
                weight_rest(n % NSLOT, upper(t, n), used(n))

        @block.scalar
        def _(act):
            act.dma_start(t.kb32[:, :], t.d_kb).then_inc(t.s_const, 16)
            act.dma_start(t.chan[:, :], t.d_chan).then_inc(t.s_const, 16)
            act.dma_start(t.pos_i[:, :], t.d_pos.partition_broadcast(P)).then_inc(t.s_const, 16)
            act.dma_start(t.sinks[:, :], t.d_sinks.partition_broadcast(P)).then_inc(t.s_const, 16)
            act.dma_start(t.wr[:, :], t.d_wr).then_inc(t.s_const, 16)

            def weight_upper(slot, hi, loaded):
                act.wait_ge(t.s_w[slot], loaded)
                act.activation(hi, t.wring[:, slot, :], ACT.Copy).then_inc(t.s_whi, 1)

            act.wait_ge(t.s_eps, 1)
            act.activation(t.nv1[:, 0:1], t.eps[:, 0:1], ACT.Sqrt).then_inc(t.s_root, 1)
            for k in range(0, KB, 2):
                act.wait_ge(t.s_xT[k // 2], 16)
                act.activation(t.uT[:, k, :], t.xT[:, k, :], ACT.Square).then_inc(t.s_sq, 1)
            for n in range(2):
                weight_upper(n, upper(t, n), 16)
            act.wait_ge(t.s_stat, 1)
            act.activation(t.rstd[:, :], bank[7][:, :], ACT.Sqrt, bias=eps).then_inc(t.s_root, 1)
            for k in range(KB):
                act.wait_ge(t.s_uT, k + 1)
                act.activation(t.u_hi[:, k, :], t.uT[:, k, :], ACT.Copy).then_inc(t.s_hi, 1)
            act.wait_ge(t.s_ang, 2)
            act.activation(t.sin[:, :], t.ang[:, :], ACT.Sin).then_inc(t.s_rope, 1)
            act.activation(t.cos[:, :], t.cos[:, :], ACT.Sin, bias=t.kf[:, K_HALFPI:K_HALFPI + 1], scale=-1.0).then_inc(t.s_rope, 1)
            with act.Fori(0, C_Q // NSLOT) as r:
                for s in range(NSLOT):
                    act.wait_ge(t.s_prod, r * 4 + s + 1)
                    if s % 2 == 0:
                        act.activation(t.cT[:, bass.ds(r * 2 + s // 2, 1), HALO:CW].rearrange("p a n -> p (a n)"), bank[s][:, :], ACT.Copy).then_inc(t.s_evac, 1)
                    else:
                        act.activation(at(t.gates, r * 2 + s // 2 + KB), bank[s][:, :], ACT.Sigmoid).then_inc(t.s_evac, 1)
                    weight_upper((s + 2) % 4, upper(t, s), (r + (s + 2) // 4) * 16 + 16)
            with act.Fori(0, KB // NSLOT) as r:
                for s in range(NSLOT):
                    act.wait_ge(t.s_prod, r * 4 + s + C_Q + 1)
                    act.activation(at(t.qT, r * 4 + s), bank[s][:, :], ACT.Copy).then_inc(t.s_evac, 1)
                    weight_upper((s + 2) % 4, upper(t, s), (r + C_Q // 4 + (s + 2) // 4) * 16 + 16)
            for n, out in ((C_KV, t.kT[:, 0, WIN:]), (C_KV + 1, t.kT[:, 1, WIN:]), (C_KV + 2, t.vT[:, :])):
                act.wait_ge(t.s_prod, n + 1)
                act.activation(out, bank[n % NSLOT][:, :], ACT.Copy).then_inc(t.s_evac, 1)
                m = n + 2 if n + 2 < SKIP else n + 3
                weight_upper(m % NSLOT, upper(t, m), 16 * loads(m))
            for n in range(C_GATE, C_COUT):
                i = n - C_GATE
                if i == I_VAR:
                    act.wait_ge(t.s_stat, 3)
                    act.activation(t.rstd[:, :], bank[7][:, :], ACT.Sqrt, bias=eps).then_inc(t.s_root, 1)
                act.wait_ge(t.s_prod, used(n))
                if i >= KB:
                    act.wait_ge(t.s_gated, i - KB + 1)
                act.activation(t.gates[:, i, :], bank[n % NSLOT][:, :], ACT.Sigmoid).then_inc(t.s_evac, 1)
                if n + 2 < C_COUT:
                    weight_upper((n + 2) % NSLOT, upper(t, n + 2), 16 * loads(n + 2))
                if i == 0:
                    act.wait_ge(t.s_vt, 1)
                    act.activation(t.v[:, 1:, :], halves(bank[4][:, :], P), ACT.Copy).then_inc(t.s_v, 1)
                for k in range(4 * (i - I_MEAN), 4 * (i - I_MEAN) + 4) if i in (I_MEAN, I_MEAN + 1) else ():
                    act.wait_ge(t.s_cent, k + 1)
                    act.activation(t.xT[:, k, :], t.cv[:, k, :], ACT.Square).then_inc(t.s_lnsq, 1)
                for k in range(4 * (i - I_VAR), 4 * (i - I_VAR) + 4) if i in (I_VAR, I_VAR + 1) else ():
                    act.wait_ge(t.s_lnt, k + 1)
                    act.activation(t.xT[:, k, :], t.cv[:, k, :], ACT.Sigmoid, bias=t.chan[:, V_BLN + k:V_BLN + k + 1],
                                   scale=t.chan[:, V_GLN + k:V_GLN + k + 1]).then_inc(t.s_lns, 1)
                    act.wait_ge(t.s_lns, k + 1)
                    act.activation(t.cv[:, k, :], t.cv[:, k, :], ACT.Identity, bias=t.chan[:, V_BLN + k:V_BLN + k + 1],
                                   scale=t.chan[:, V_GLN + k:V_GLN + k + 1]).then_inc(t.s_lna, 1)
            def exponentials(u):
                act.wait_ge(t.s_max, u + 1)
                for x in range(4):
                    act.activation(t.sm[:, u % 2, x, :], t.sm[:, u % 2, x, :], ACT.Exp, bias=t.negm[:, u, x:x + 1],
                                   scale=SCALE, accum_out=t.rsum[:, u, x:x + 1]).then_inc(t.s_exp, 1)
                act.activation(t.esink[:, u, :], t.esink[:, u, :], ACT.Exp).then_inc(t.s_exp, 1)

            exponentials(0)
            for k in range(KB):
                act.wait_ge(t.s_ln, k + 1)
                act.activation(t.cv_hi[:, k, :], t.cv[:, k, :], ACT.Copy).then_inc(t.s_hi, 1)
            act.wait_ge(t.s_rot, KB + KV)
            act.wait_ge(t.s_scat, 48)
            weight_upper(C_COUT % NSLOT, upper(t, C_COUT), 16 * loads(C_COUT))
            exponentials(1)
            for u in range(NU):
                act.wait_ge(t.s_pt, 2 * u + 2)
                if u:
                    act.wait_ge(t.s_pv, u)
                act.activation(t.pT[:, 0, :, :], halves(bank[4][:, :], P), ACT.Copy).then_inc(t.s_ept0, 1)
                act.wait_ge(t.s_pv, u + 1)
                act.activation(heads_of(t.o_hi, u), halves(bank[6][:, 0:2 * WIN], WIN), ACT.Copy).then_inc(t.s_eo, 1)
                if u + 2 < NU:
                    exponentials(u + 2)
                if u == 0:
                    weight_upper((C_COUT + 1) % NSLOT, upper(t, C_COUT + 1), 16 * loads(C_COUT + 1))
                elif u % 2 and u > 1:
                    n = C_COUT + (u + 1) // 2
                    act.wait_ge(t.s_prod, used(n - 2))
                    weight_upper(n % NSLOT, upper(t, n), 16 * loads(n))
            n = C_AOUT + 1
            act.wait_ge(t.s_prod, used(n - 2))
            weight_upper(n % NSLOT, upper(t, n), 16 * loads(n))
            act.wait_ge(t.s_pt, 2 * NU)
            act.dma_start(t.gffn[:, :], t.d_gffn.partition_broadcast(P)).then_inc(t.s_late, 16)
            act.dma_start(t.b2[:, :], t.d_b2).then_inc(t.s_late, 16)
            act.dma_start(t.b1all[:, :], t.d_b1).then_inc(t.s_late, 16)
            for n in range(C_AOUT + 2, N_CHUNK):
                act.wait_ge(t.s_prod, used(n - 2))
                weight_upper(n % NSLOT, upper(t, n), 16 * loads(n))
                k = n - C_AOUT - 2
                if k < KB:
                    act.wait_ge(t.s_merge, KB + k + 1)
                    act.activation(t.mix_hi[:, k, :], t.mix[:, k, :], ACT.Copy).then_inc(t.s_hi, 1)
            act.activation(t.nv1[:, 0:1], t.eps[:, 0:1], ACT.Sqrt).then_inc(t.s_root, 1)
            for j in range(TT):
                act.wait_ge(t.s_h, 2 * j + 2)
                if j:
                    act.wait_ge(t.s_ss, j)
                act.activation(t.u2[:, j, :], t.h[:, j, :], ACT.Square, accum_out=t.ss[:, j:j + 1]).then_inc(t.s_ss, 1)
                act.wait_ge(t.s_ss, j + 1)
                act.activation(t.ss[:, j:j + 1], t.ss[:, j:j + 1], ACT.Sqrt, bias=eps, scale=1.0 / D).then_inc(t.s_root, 1)
            for j in range(TT):
                act.wait_ge(t.s_ut, 2 * j + 1)
                act.activation(t.u2T[:, 0:4, j * P:(j + 1) * P], halves(bank[2 * (j % 2)][:, :], P), ACT.Copy).then_inc(t.s_eut0, 1)
            act.wait_ge(t.s_top, 1)
            for j in range(TT):
                act.activation(t.gexp[:, j, :], t.logits[:, j, :], ACT.Exp, bias=t.nv1[:, j:j + 1]).then_inc(t.s_gexp, 1)

        @block.tensor
        def _(pe):
            def parts(out, lhs_hi, lhs_lo, rhs_hi, rhs_lo, start, stop):
                for i, (a, b) in enumerate(((lhs_hi, rhs_hi), (lhs_lo, rhs_hi), (lhs_hi, rhs_lo))):
                    mm = pe.matmul(out, a, b, start=start and i == 0, stop=stop and i == 2)
                return mm

            def product(out, s, hi, count, rhs_hi, rhs_lo, ks=range(KB), ready=False):
                pe.wait_ge(t.s_wlo, count)
                for k in ks:
                    if ready:
                        pe.wait_ge(t.s_lo, k + 1)
                    mm = parts(out, hi[:, k * P:(k + 1) * P], t.wlo[:, s, k * P:(k + 1) * P], rhs_hi[:, k, :], rhs_lo[:, k, :], k == 0, k == KB - 1)
                if KB - 1 in ks:
                    mm.then_inc(t.s_prod, 1)

            def scores(u):
                hp, blk, kv = (u // 8) * 4 + (u % 2) * 2, (u // 2) % 4, u // 8
                if u < 2:
                    pe.wait_ge(t.s_evac, used(C_COUT - 3) if u == 0 else used(C_COUT - 1))
                    pe.wait_ge(t.s_rot, KV + 2 if u == 0 else KV + KB)
                    pe.wait_ge(t.s_zero, 3)
                if u >= 2:
                    pe.wait_ge(t.s_masked, 2 * (u - 1))
                for x in range(2):
                    for half in range(2):
                        rows = slice(half * HD, half * HD + HD)
                        mm = pe.matmul(bank[2 * (u % 2) + half][:, x * 2 * WIN:(x + 1) * 2 * WIN], t.qT[rows, hp + x, blk * WIN:(blk + 1) * WIN],
                                       t.kT[rows, kv, blk * WIN:(blk + 2) * WIN], start=True, stop=True)
                mm.then_inc(t.s_score, 1)

            pe.wait_ge(t.s_kf, 16)
            for k in range(KB):
                pe.wait_ge(t.s_sq if k % 2 == 0 else t.s_sqodd, k // 2 + 1)
                mm = pe.matmul(bank[7][:, :], t.kf[:, K_MEAN:K_MEAN + P], t.uT[:, k, :], start=(k == 0), stop=(k == KB - 1))
            mm.then_inc(t.s_stat, 1)

            for s in range(NSLOT):
                product(bank[s][:, :], s, upper(t, s), s + 1, t.u_hi, t.u_lo, ready=(s == 0))
            with pe.Fori(1, C_KV // NSLOT) as r:
                for s in range(NSLOT):
                    pe.wait_ge(t.s_evac, r * 4 + s - 3)
                    product(bank[s][:, :], s, upper(t, s), r * 4 + s + 1, t.u_hi, t.u_lo)
            for n in range(C_KV, SKIP):
                pe.wait_ge(t.s_evac, n - 3)
                product(bank[n % NSLOT][:, :], n % NSLOT, upper(t, n), used(n), t.u_hi, t.u_lo)
            for n in range(C_GATE, C_COUT):
                s, i = n % NSLOT, n - C_GATE
                if i == I_MEAN:
                    pe.wait_ge(t.s_csum, KB - 1)
                    pe.matmul(bank[6][:, :], t.kf[:, K_MEAN:K_MEAN + P], t.csum[:, 0, :], start=True, stop=True).then_inc(t.s_stat, 1)
                if i == I_VAR:
                    pe.wait_ge(t.s_csum, 2 * (KB - 1))
                    pe.matmul(bank[7][:, :], t.kf[:, K_MEAN:K_MEAN + P], t.csum[:, 1, :], start=True, stop=True).then_inc(t.s_stat, 1)
                pe.wait_ge(t.s_evac, n - 3 if n < C_GATE + 3 else n - NSLOT)
                if n == C_COUT - 1:
                    scores(0)
                product(bank[s][:, :], s, upper(t, n), used(n), t.u_hi, t.u_lo)
                if i == 0:
                    pe.wait_ge(t.s_evac, SKIP)
                    for j in range(TT):
                        mm = pe.transpose(bank[4][:, j * P:(j + 1) * P], t.vT[:, j * P:(j + 1) * P], ident)
                    mm.then_inc(t.s_vt, 1)
                if i >= I_MEAN:
                    for j in range(2 * (i - I_MEAN), min(2 * (i - I_MEAN) + 2, KB + KV)):
                        if j >= 2:
                            pe.wait_ge(t.s_rot, j - 1)
                        else:
                            pe.wait_ge(t.s_v, 1)
                        pe.matmul(bank[4 + j % 2][:, :], t.kf[:, K_ROT:K_ROT + P], rotated(t, j), start=True, stop=True).then_inc(t.s_swap, 1)

            def turn_probs(u):
                pe.wait_ge(t.s_prob, u + 1)
                for kt in (1, 0):
                    if u:
                        pe.wait_ge((t.s_ept0, t.s_ept1)[kt], u)
                    for x in range(4):
                        mm = pe.transpose(bank[4 + kt][:, x * P:(x + 1) * P], t.sm[:, u % 2, x, kt * P:(kt + 1) * P], ident)
                    mm.then_inc(t.s_pt, 1)

            def values(u):
                blk, kv = (u // 2) % 4, u // 8
                pe.wait_ge(t.s_ept0, u + 1)
                pe.wait_ge(t.s_ept1, u + 1)
                if u:
                    pe.wait_ge(t.s_olo, u)
                for half in range(2):
                    for kt in range(2):
                        mm = pe.matmul(bank[6][half * HD:(half + 1) * HD, 0:2 * WIN], t.v[:, blk + kt, kv * HD:(kv + 1) * HD],
                                       t.pT[:, kt, 2 * half:2 * half + 2, :], start=(kt == 0), stop=(kt == 1))
                mm.then_inc(t.s_pv, 1)

            def half_product(x):
                n = C_COUT + x // 2
                if x < 2:
                    pe.wait_ge(t.s_lo, KB + 4 * x + 4)
                elif x % 2 == 0:
                    pe.wait_ge(t.s_merge, x // 2)
                product(bank[7][:, :], n % NSLOT, upper(t, n), used(n), t.cv_hi, t.cv_lo, ks=range(x % 2 * 4, x % 2 * 4 + 4))

            scores(1)
            for u in range(NU):
                if u + 2 < NU:
                    scores(u + 2)
                turn_probs(u)
                if u:
                    half_product(u - 1)
                values(u)
            half_product(NU - 1)

            pe.wait_ge(t.s_masked, 2 * NU)
            pe.wait_ge(t.s_olo, NU)
            for n in range(C_AOUT, C_WOUT):
                if n >= C_AOUT + NSLOT:
                    pe.wait_ge(t.s_merge, KB + n - C_AOUT - NSLOT + 1)
                product(bank[n % NSLOT][:, :], n % NSLOT, upper(t, n), used(n), t.o_hi, t.o_lo)
            pe.wait_ge(t.s_merge, 2 * KB)
            for k in range(KB):
                n = C_WOUT + k
                pe.wait_ge(t.s_wlo, used(n))
                pe.wait_ge(t.s_lo, 2 * KB + k + 1)
                for j in range(TT):
                    for c in range(2):
                        tok, col = slice(j * P, (j + 1) * P), slice(c * SEQ, (c + 1) * SEQ)
                        mm = parts(bank[2 * j + c][:, :], t.mix_hi[:, k, tok], t.mix_lo[:, k, tok], upper(t, n)[:, col], t.wlo[:, n % NSLOT, col],
                                   k == 0, k == KB - 1)
                    if k == KB - 1 and j < TT - 1:
                        mm.then_inc(t.s_rows, 1)
                mm.then_inc(t.s_prod, 1)
            for j in range(TT):
                pe.wait_ge(t.s_u2, j + 1)
                if j == 0:
                    pe.wait_ge(t.s_h, 2 * TT)
                if j >= 2:
                    pe.wait_ge(t.s_eut0, j - 1)
                    pe.wait_ge(t.s_eut1, j - 1)
                for c in range(2):
                    for x in range(4):
                        k = 4 * c + x
                        mm = pe.transpose(bank[2 * (j % 2) + c][:, x * P:(x + 1) * P], t.u2[:, j, k * P:(k + 1) * P], ident)
                    mm.then_inc(t.s_ut, 1)
            pe.wait_ge(t.s_eut0, TT)
            pe.wait_ge(t.s_eut1, TT)
            for k in range(KB):
                for j in range(TT):
                    mm = pe.matmul(bank[4][E * j:E * (j + 1), 0:P], t.wr[:, k * E:(k + 1) * E], t.u2T[:, k, j * P:(j + 1) * P],
                                   start=(k == 0), stop=(k == KB - 1))
            mm.then_inc(t.s_route, 1)
            pe.wait_ge(t.s_lt, 1)
            pe.transpose(bank[5][:, 0:P], t.lT[:, :], ident).then_inc(t.s_route, 1)
            pe.wait_ge(t.s_sel, 1)
            selb = t.selb[:, :, :]
            pe.matmul(halves(bank[6][:, 0:TT * E], E), t.kb[:, B_TRI:B_TRI + P], selb, start=True, stop=False)
            for j in range(TT - 1):
                for i in range(j + 1, TT):
                    mm = pe.matmul(bank[6][:, i * E:(i + 1) * E], t.kb[:, B_ONE:B_ONE + P], t.selb[:, j, :], start=False, stop=(j == TT - 2))
            mm.then_inc(t.s_route, 1)
            for j in range(TT):
                mm = pe.matmul(bank[7][:, 0:E], t.kb[:, B_ONE:B_ONE + P], t.selb[:, j, :], start=(j == 0), stop=(j == TT - 1))
            mm.then_inc(t.s_route, 1)
            pe.wait_ge(t.s_gate, 1)
            pe.transpose(bank[5][:, P:2 * P], t.gate[:, :, :].rearrange("p a n -> p (a n)"), ident).then_inc(t.s_route, 1)
            pe.wait_ge(t.s_gT, TT)
            pe.wait_ge(t.s_late, 48)
            for x in range(TT):
                gated_bias(pe, t, x)
            pe.wait_ge(t.s_list, 1)
            for c in range(LIST):
                mm = pe.matmul(bank[7][0:1, c * P:(c + 1) * P], t.listcol[:, c:c + 1], ident, start=True, stop=True)
            mm.then_inc(t.s_listrow, 1)
            pe.wait_ge(t.s_diag, 1)
            pe.matmul(bank[4][:, 0:P], t.kf[:, K_ONE:K_ONE + P], t.diag[:, :], start=True, stop=True).then_inc(t.s_first, 1)

        @block.vector
        def _(dve):
            step = Chain(dve, t.s_dve)
            dve.memset(t.eps[:, :], EPS).then_inc(t.s_eps, 1)
            for k in range(1, KB, 2):
                dve.wait_ge(t.s_xT[k // 2], 16)
                dve.tensor_tensor(t.uT[:, k, :], t.xT[:, k, :], t.xT[:, k, :], ALU.mult).then_inc(t.s_sqodd, 1)
            dve.wait_ge(t.s_const, 16 * 5)
            dve.wait_ge(t.s_kf, 16)
            dve.wait_ge(t.s_root, 2)
            step.link(dve.reciprocal(t.rstd[:, :], t.rstd[:, :]))
            for k in range(KB):
                dve.scalar_tensor_tensor(t.uT[:, k, :], t.xT[:, k, :], t.chan[:, V_GMIX + k:V_GMIX + k + 1], t.rstd[:, :],
                                         ALU.mult, ALU.mult).then_inc(t.s_uT, 1)
            step.link(dve.tensor_copy(t.kb[:, :], t.kb32[:, :]))
            step.link(dve.tensor_copy(t.ang[:, :], t.pos_i[:, :]))
            step.link(dve.tensor_scalar(t.ang[:, :], t.ang[:, :], t.kf[:, K_FREQ:K_FREQ + 1], None, ALU.mult))
            step.link(dve.tensor_scalar(t.cos[:, :], t.ang[:, :], 1.0 / TWO_PI, ROUND, ALU.mult, ALU.add))
            step.link(dve.tensor_scalar(t.cos[:, :], t.cos[:, :], ROUND, None, ALU.subtract))
            for part in (PI_A, PI_B, PI_C):
                step.link(dve.scalar_tensor_tensor(t.ang[:, :], t.cos[:, :], -part, t.ang[:, :], ALU.mult, ALU.add))
            step.link(dve.tensor_scalar(t.ang[:, :], t.ang[:, :], 3.1415925, -3.1415925, ALU.min, ALU.max))
            dve.tensor_scalar(t.cos[:, :], t.ang[:, :], -1.0, None, ALU.mult).then_inc(t.s_ang, 1)
            dve.wait_ge(t.s_ang, 1)
            dve.tensor_tensor(t.cos[:, :], t.cos[:, :], t.ang[:, :], ALU.max).then_inc(t.s_ang, 1)
            dve.wait_ge(t.s_zero, 1)
            with dve.Fori(0, KB) as i:
                conv = Chain(dve, t.s_tap)
                base = i * (TAPS + 1)
                row = at(t.cv, i)

                def tap(k):
                    return t.cT[:, bass.ds(i, 1), k:k + SEQ].rearrange("p a n -> p (a n)")

                def weight(k):
                    return t.chan[:, bass.ds(i * TAPS + V_DW + k, 1)]

                dve.wait_ge(t.s_evac, i * 2 + 2)
                conv.link(dve.tensor_tensor(tap(HALO), tap(HALO), at(t.gates, i + KB), ALU.mult), base)
                conv.add(dve.tensor_scalar(row, tap(0), weight(0), t.chan[:, bass.ds(i + V_BDW, 1)], ALU.mult, ALU.add))
                conv.add(dve.tensor_scalar(t.odd[:, :], tap(1), weight(1), None, ALU.mult))
                for k in range(2, TAPS):
                    acc = t.odd[:, :] if k % 2 else row
                    conv.sync(1, base)
                    conv.add(dve.scalar_tensor_tensor(acc, tap(k), weight(k), acc, ALU.mult, ALU.add))
                conv.sync(0, base)
                assert conv.n == TAPS + 1
                dve.tensor_tensor(row, row, t.odd[:, :], ALU.add).then_inc(t.s_conv, 1)
                dve.wait_ge(t.s_conv, i + 1)
                dve.sem_inc(t.s_gated, 1)
            dve.wait_ge(t.s_stat, 2)
            for k in range(KB):
                dve.tensor_tensor(t.cv[:, k, :], t.cv[:, k, :], bank[6][:, :], ALU.subtract).then_inc(t.s_cent, 1)
            dve.wait_ge(t.s_rope, 2)
            dve.wait_ge(t.s_evac, C_KV + KV)
            for i in range(KB + KV):
                x = rotated(t, i)
                dve.wait_ge(t.s_swap, i + 1)
                step.link(dve.tensor_tensor(t.odd[:, :], bank[4 + i % 2][:, :], t.sin[:, :], ALU.mult))
                dve.wait_ge(t.s_xcos, i + 1)
                dve.tensor_tensor(x, t.xcos[:, i % 2, :], t.odd[:, :], ALU.add).then_inc(t.s_rot, 1)
                dve.wait_ge(t.s_rot, i + 1)
                if i == 2 * (I_VAR - I_MEAN) - 1:
                    dve.wait_ge(t.s_cent, KB)
                    dve.wait_ge(t.s_root, 3)
                    step.link(dve.reciprocal(t.rstd[:, :], t.rstd[:, :]))
                    for k in range(KB):
                        dve.tensor_tensor(t.cv[:, k, :], t.cv[:, k, :], t.rstd[:, :], ALU.mult).then_inc(t.s_lnt, 1)

            def masked(u):
                blk = (u // 2) % 4
                mask = t.kf[:, K_MASK + 256 * (blk == 0):K_MASK + 256 * (blk == 0) + 256].unsqueeze(1).to_broadcast([P, 2, 2 * WIN])
                dve.wait_ge(t.s_score, u + 1)
                if u == 0:
                    dve.wait_ge(t.s_prod, used(C_COUT - 1))
                if u >= 2:
                    dve.wait_ge(t.s_pt, 2 * (u - 1))
                for half in range(2):
                    dve.tensor_tensor(t.sm[:, u % 2, 2 * half:2 * half + 2, :], halves(bank[2 * (u % 2) + half][:, :], 2 * WIN), mask,
                                      ALU.add).then_inc(t.s_masked, 1)
                dve.wait_ge(t.s_masked, 2 * (u + 1))
                mx, sinks = t.mx[:, u, :], t.sinks[:, 4 * (u // 8 * 2 + u % 2):4 * (u // 8 * 2 + u % 2) + 4]
                step.link(dve.tensor_reduce(mx, t.sm[:, u % 2, :, :], AX.X, ALU.max))
                step.link(dve.scalar_tensor_tensor(mx, mx, SCALE, sinks, ALU.mult, ALU.max))
                step.link(dve.tensor_scalar(t.negm[:, u, :], mx, -1.0, None, ALU.mult))
                dve.tensor_tensor(t.esink[:, u, :], sinks, t.negm[:, u, :], ALU.add).then_inc(t.s_max, 1)

            def output_rest(u):
                dve.wait_ge(t.s_eo, u + 1)
                dve.tensor_tensor(heads_of(t.o_lo, u), halves(bank[6][:, 0:2 * WIN], WIN), heads_of(t.o_hi, u).bitcast(F32), ALU.subtract).then_inc(t.s_olo, 1)

            def gate_conv(k):
                dve.wait_ge(t.s_prod, used(C_COUT + k))
                dve.tensor_tensor(t.mix[:, k, :], bank[7][:, :], t.gates[:, k, :], ALU.mult).then_inc(t.s_merge, 1)

            def probabilities(u):
                dve.wait_ge(t.s_exp, 5 * (u + 1))
                step.link(dve.tensor_tensor(t.rsum[:, u, :], t.rsum[:, u, :], t.esink[:, u, :], ALU.add))
                step.link(dve.reciprocal(t.rsum[:, u, :], t.rsum[:, u, :]))
                for x in range(4):
                    step.add(dve.tensor_scalar(t.sm[:, u % 2, x, :], t.sm[:, u % 2, x, :], t.rsum[:, u, x:x + 1], None, ALU.mult))
                step.sync()
                dve.sem_inc(t.s_prob, 1)

            def silu(k):
                dve.wait_ge(t.s_lna, k + 1)
                dve.tensor_tensor(t.cv[:, k, :], t.cv[:, k, :], t.xT[:, k, :], ALU.mult).then_inc(t.s_ln, 1)

            for k in range(KB // 2):
                silu(k)
            masked(0)
            for k in range(KB // 2, KB):
                silu(k)
            probabilities(0)
            masked(1)
            for u in range(NU):
                dve.wait_ge(t.s_pt, 2 * u + 1)
                if u:
                    dve.wait_ge(t.s_pv, u)
                dve.tensor_copy(t.pT[:, 1, :, :], halves(bank[5][:, :], P)).then_inc(t.s_ept1, 1)
                if u + 2 < NU:
                    masked(u + 2)
                if u + 1 < NU:
                    probabilities(u + 1)
                output_rest(u)
                if u % 2 == 0 and u:
                    gate_conv(u // 2 - 1)
            gate_conv(KB - 1)
            dve.wait_ge(t.s_merge, KB)
            for k in range(KB):
                dve.wait_ge(t.s_prod, used(C_AOUT + k))
                step.link(dve.tensor_tensor(t.odd[:, :], bank[(C_AOUT + k) % NSLOT][:, :], t.gates[:, KB + k, :], ALU.mult))
                dve.tensor_tensor(t.mix[:, k, :], t.mix[:, k, :], t.odd[:, :], ALU.add).then_inc(t.s_merge, 1)
                dve.wait_ge(t.s_merge, KB + k + 1)
            dve.wait_ge(t.s_x, 16)
            def residual(j):
                if j < TT - 1:
                    dve.wait_ge(t.s_rows, j + 1)
                else:
                    dve.wait_ge(t.s_prod, used(N_CHUNK - 1))
                for c in range(2):
                    dve.tensor_tensor(t.h[:, j, c * SEQ:(c + 1) * SEQ], t.h[:, j, c * SEQ:(c + 1) * SEQ], bank[2 * j + c][:, :], ALU.add).then_inc(t.s_h, 1)

            def normed(j):
                dve.wait_ge(t.s_root, 5 + j)
                step.link(dve.reciprocal(t.ss[:, j:j + 1], t.ss[:, j:j + 1]))
                dve.scalar_tensor_tensor(t.u2[:, j, :], t.h[:, j, :], t.ss[:, j:j + 1], t.gffn[:, :], ALU.mult, ALU.mult).then_inc(t.s_u2, 1)

            dve.wait_ge(t.s_late, 48)
            for j in range(TT):
                residual(j)
                if j:
                    dve.wait_ge(t.s_h, 2 * j)
                    normed(j - 1)
            dve.wait_ge(t.s_h, 2 * TT)
            normed(TT - 1)
            for j in range(TT):
                dve.wait_ge(t.s_ut, 2 * j + 2)
                dve.tensor_copy(t.u2T[:, 4:8, j * P:(j + 1) * P], halves(bank[2 * (j % 2) + 1][:, :], P)).then_inc(t.s_eut1, 1)
            dve.wait_ge(t.s_route, 1)
            dve.tensor_scalar(t.lT[:, :], bank[4][:, 0:P], t.chan[:, V_BR:V_BR + 1], None, ALU.add).then_inc(t.s_lt, 1)
            dve.wait_ge(t.s_route, 2)
            step.link(dve.tensor_copy(t.logits[:, :, :], halves(bank[5][:, 0:P], E)))
            for j in range(TT):
                step.add(dve.max(t.top[:, j, :], t.logits[:, j, :]))
            step.sync()
            dve.tensor_scalar(t.nv1[:, :].unsqueeze(2), t.top[:, :, 0:1], -1.0, None, ALU.mult).then_inc(t.s_top, 1)
            v4 = t.top[:, :, TOPK - 1:TOPK].to_broadcast([P, TT, E])
            step.add(dve.tensor_tensor(t.sel[:, :, :], t.logits[:, :, :], v4, ALU.is_gt))
            step.link(dve.tensor_tensor(t.tie[:, :, :], t.logits[:, :, :], v4, ALU.is_equal))
            step.link(dve.tensor_reduce(t.room[:, :], t.sel[:, :, :], AX.X, ALU.add))
            step.link(dve.tensor_scalar(t.room[:, :], t.room[:, :], -1.0, float(TOPK), ALU.mult, ALU.add))
            for j in range(TT):
                step.add(dve.tensor_tensor_scan(t.rank[:, j, :], t.kf[:, K_ONE:K_ONE + E], t.tie[:, j, :], 0.0, ALU.mult, ALU.add))
            step.sync()
            step.link(dve.tensor_tensor(t.rank[:, :, :], t.rank[:, :, :], t.room[:, :].unsqueeze(2).to_broadcast([P, TT, E]), ALU.is_le))
            step.link(dve.tensor_tensor(t.tie[:, :, :], t.tie[:, :, :], t.rank[:, :, :], ALU.mult))
            step.link(dve.tensor_tensor(t.sel[:, :, :], t.sel[:, :, :], t.tie[:, :, :], ALU.add))
            dve.tensor_copy(t.selb[:, :, :], t.sel[:, :, :]).then_inc(t.s_sel, 1)
            dve.wait_ge(t.s_gexp, TT)
            step.link(dve.tensor_tensor(t.gate[:, :, :], t.gexp[:, :, :], t.sel[:, :, :], ALU.mult))
            step.link(dve.tensor_reduce(t.room[:, :], t.gate[:, :, :], AX.X, ALU.add))
            step.link(dve.reciprocal(t.room[:, :], t.room[:, :]))
            dve.tensor_tensor(t.gate[:, :, :], t.gate[:, :, :], t.room[:, :].unsqueeze(2).to_broadcast([P, TT, E]), ALU.mult).then_inc(t.s_gate, 1)
            dve.wait_ge(t.s_route, 5)
            for j in range(TT):
                dve.tensor_scalar(t.gT[:, j, :], bank[5][:, P:2 * P], t.kf[:, K_TILE + j:K_TILE + j + 1], None, ALU.mult).then_inc(t.s_gT, 1)
            dve.wait_ge(t.s_route, 4)
            step.link(dve.tensor_scalar(t.tie[:, :, :], t.sel[:, :, :], -UNROUTED, UNROUTED, ALU.mult, ALU.add))
            step.add(dve.tensor_tensor(t.place[:, :, :], halves(bank[6][:, 0:TT * E], E), t.tie[:, :, :], ALU.add))
            step.link(dve.tensor_copy(t.cnt[:, :], bank[7][:, 0:E]))
            step.link(dve.tensor_scalar(t.more[:, :], t.cnt[:, :], float(CAP), None, ALU.is_gt))
            for m in range(2, -(-SEQ // CAP)):
                step.link(dve.scalar_tensor_tensor(t.more[:, :], t.cnt[:, :], float(CAP * m), t.more[:, :], ALU.is_gt, ALU.add))
            step.link(dve.tensor_tensor_scan(t.run[:, :], t.kf[:, K_ONE:K_ONE + E], t.more[:, :], 0.0, ALU.mult, ALU.add))
            extra, own, before, isx = (t.tmp[:, c:c + 1] for c in range(4))
            pnum = t.kf[:, K_P:K_P + 1]
            step.link(dve.tensor_scalar(extra, pnum, float(E), None, ALU.subtract))
            step.add(dve.tensor_scalar(isx, pnum, float(E), None, ALU.is_ge))
            step.link(dve.tensor_scalar(t.below[:, :], t.run[:, :], extra, None, ALU.is_le))
            step.link(dve.tensor_reduce(own, t.below[:, :], AX.X, ALU.add))
            step.link(dve.tensor_tensor(t.below[:, :], t.below[:, :], t.more[:, :], ALU.mult))
            step.link(dve.tensor_reduce(before, t.below[:, :], AX.X, ALU.add))
            step.link(dve.tensor_scalar(own, own, float(E - 1), pnum, ALU.min, ALU.subtract))
            step.link(dve.tensor_tensor(own, own, isx, ALU.mult))
            step.add(dve.tensor_scalar(t.listcol[:, 0:1], own, pnum, None, ALU.add))
            step.link(dve.tensor_tensor(extra, extra, before, ALU.subtract))
            step.link(dve.tensor_scalar(extra, extra, 1.0, float(CAP), ALU.add, ALU.mult))
            step.link(dve.tensor_tensor(extra, extra, isx, ALU.mult))
            step.link(dve.tensor_scalar(isx, pnum, t.run[:, E - 1:E], float(E), ALU.subtract, ALU.is_ge))
            step.link(dve.scalar_tensor_tensor(extra, isx, NOWHERE, extra, ALU.mult, ALU.add))
            step.link(dve.tensor_scalar(before, t.run[:, E - 1:E], 0.5, (E + 1) / 2 - 0.25, ALU.mult, ALU.add))
            step.link(dve.tensor_scalar(before, before, ROUND, None, ALU.add))
            step.link(dve.tensor_scalar(before, before, ROUND, None, ALU.subtract))
            step.add(dve.tensor_copy(t.listcol[:, 1:2], before))
            step.link(dve.tensor_scalar(own, own, pnum, None, ALU.add))
            step.link(dve.tensor_scalar(t.below[:, :], t.kf[:, K_E:K_E + E], own, None, ALU.is_equal))
            step.link(dve.tensor_tensor(t.below[:, :], t.below[:, :], t.cnt[:, :], ALU.mult))
            step.link(dve.tensor_reduce(own, t.below[:, :], AX.X, ALU.add))
            step.link(dve.tensor_tensor(own, own, extra, ALU.subtract))
            step.link(dve.tensor_scalar(t.listcol[:, 2:3], own, 0.0, None, ALU.max))
            dve.sem_inc(t.s_list, 1)
            dve.tensor_scalar(t.diag[:, :], ident, extra, None, ALU.mult).then_inc(t.s_diag, 1)
            dve.wait_ge(t.s_listrow, 1)
            step.link(dve.tensor_copy(t.lists[:, :], bank[7][0:1, 0:LIST * P]))
            for j in range(TT):
                step.add(dve.tensor_copy(t.bring[:, j, :, 0:3], t.kb[:, B_TOK + 3 * j:B_TOK + 3 * j + 3].unsqueeze(1).to_broadcast([P, E, 3])))
            dve.wait_ge(t.s_gate, 1)
            dve.wait_ge(t.s_gT, TT)
            step.link(dve.tensor_copy(t.bring[:, :, :, 3], t.gate[:, :, :]))
            step.link(dve.tensor_tensor(t.gate[:, :, :], t.gate[:, :, :], t.bring[:, :, :, 3], ALU.subtract))
            step.link(dve.tensor_copy(t.bring[:, :, :, 4], t.gate[:, :, :]))
            step.link(dve.tensor_tensor(t.gate[:, :, :], t.gate[:, :, :], t.bring[:, :, :, 4], ALU.subtract))
            step.link(dve.tensor_copy(t.bring[:, :, :, 5], t.gate[:, :, :]))
            dve.wait_ge(t.s_first, 1)
            dve.tensor_copy(t.first[:, :], bank[4][:, 0:P]).then_inc(t.s_efirst, 1)


def mixture(nc, t):
    bank = t.bank
    ident = t.kf[:, K_ID:K_ID + P]
    PT, PX, PY = (5, 0, 1), (3, 4), (6, 7)

    with nc.Block() as block:

        def expert_of(eng, i):
            return eng.value_load(t.lists[0:1, bass.ds(i, 1)], min_val=0, max_val=E - 1)

        def pair_count(eng):
            return eng.value_load(t.lists[0:1, P:P + 1], min_val=E // 2, max_val=(E + MORE + 1) // 2)

        @block.sync
        def _(sp):
            pairs = pair_count(sp)

            def load_w1(i, e):
                for k in range(KB):
                    sp.wait_ge(t.s_w1used, i * KB + k + 1)
                    sp.dma_start(t.w1[:, k, :], t.d_w1[bass.ds(e, 1), k * P:(k + 1) * P, :].rearrange("a p n -> (a p) n")).then_inc(t.s_w1[k], 16)

            def load_w2(j, e, side):
                sp.dma_start(t.w2p[:, side, j, :, :],
                             t.d_w2[bass.ds(e, 1), j * FC:(j + 1) * FC, :].rearrange("e (a p) n -> p (e a) n", p=P)).then_inc(t.s_w2[j], 16)

            sp.dma_start(t.gfin[:, :], t.d_gfin.partition_broadcast(P)).then_inc(t.s_fin, 16)
            e = expert_of(sp, 1)
            for j in range(2):
                load_w2(j, e, 1)
            for j in range(TT):
                sp.wait_ge(t.s_acc, TT + j + 1)
                sp.dma_start(t.d_acc[j * P:(j + 1) * P, :], t.h[:, j, :]).then_inc(t.s_accout, 16)
            sp.wait_ge(t.s_accout, 16 * TT)
            for j in range(2, 4):
                load_w2(j, e, 1)
            load_w1(0, e)
            with sp.Fori(1, pairs) as r:
                for side in range(2):
                    i = r * 2 + (side - 1)
                    e = expert_of(sp, i + 1)
                    for j in range(4):
                        sp.wait_ge(t.s_w2used, i * 4 + (j - 3))
                        sp.wait_ge(t.s_w2[j], i * 16 + 16)
                        load_w2(j, e, side)
                    load_w1(i, e)

        @block.gpsimd
        def _(pool):
            n = pair_count(pool) * 2

            def gather():
                pool.indirect_dma_start(out=t.xg[:, :], out_offset=None, in_=t.d_u2, in_offset=bass.IndirectOffsetOnAxis(ap=t.gidx[:, 0:1], axis=0)).then_inc(t.s_gather, 16)

            pool.wait_ge(t.s_gidx, 1)
            gather()
            pool.wait_ge(t.s_accout, 16 * TT)
            with pool.Fori(0, n) as i:
                pool.wait_ge(t.s_gidx, i + 2)
                pool.wait_ge(t.s_xt, i * 2 + 2)
                pool.sem_inc(t.s_go, 1)
                gather()
                for g in range(NG):
                    pool.wait_ge(t.s_ysb, i * NG + g + 2)
                    pool.wait_ge(t.s_sidx, i + 1)
                    pool.sem_inc(t.s_go, 1)
                    pool.indirect_dma_start(out=t.d_acc4, out_offset=bass.IndirectOffsetOnAxis(ap=t.sidx[:, g:g + 1], axis=0), in_=t.ysb[:, g, :],
                                            in_offset=None, compute_op=ALU.add).then_inc(t.s_scat, 16)
            pool.wait_ge(t.s_gather, n * 16 + 16)
            pool.wait_ge(t.s_scat, n * 48 + 48)

        @block.scalar
        def _(act):
            n = pair_count(act) * 2

            def turn(i):
                act.wait_ge(t.s_xt, i * 2 + 1)
                act.activation(t.xe[:, 0:4, :], halves(bank[PX[0]][:, 0:4 * CAP], CAP), ACT.Copy).then_inc(t.s_xe, 1)

            turn(0)
            with act.Fori(0, n) as i:
                act.wait_ge(t.s_spread, i + 1)
                act.wait_ge(t.s_hfree, i * NG + NG)
                for half in range(2):
                    act.activation(t.b1[:, half * FC:(half + 1) * FC], bank[PY[half]][:, FC:], ACT.Copy).then_inc(t.s_b1, 1)
                for g in range(NG):
                    act.wait_ge(t.s_glu, i * NG + g + 1)
                    act.activation(t.sig[:, g, :], t.hb[:, g, 0:FC], ACT.Sigmoid, scale=ALPHA).then_inc(t.s_sig, 1)
                turn(i + 1)
                act.wait_ge(t.s_scat, i * 48 + 48)
                for g in range(NG):
                    if g < NG - 1:
                        act.wait_ge(t.s_y, i * (NG - 1) + g + 1)
                    else:
                        act.wait_ge(t.s_w2used, i * 4 + 4)
                    act.activation(t.ysb[:, g, :], bank[PY[g % 2]][:, 0:FC], ACT.Copy, scale=t.sgate[:, bass.ds(i * NG + g, 1)]).then_inc(t.s_ysb, 1)

        @block.tensor
        def _(pe):
            pairs = pair_count(pe)

            def dispatch(i):
                e = expert_of(pe, i)
                pe.wait_ge(t.s_hot, i + 1)
                for g in range(NG):
                    for j in range(TT):
                        pe.matmul(bank[5][:, 8 * g:8 * g + 6], t.hot[:, j, g * P:(g + 1) * P], t.bring[:, j, bass.ds(e, 1), :].rearrange("p a n -> p (a n)"),
                                  start=(j == 0), stop=(j == TT - 1))
                for j in range(TT):
                    mm = pe.matmul(bank[5][0:CAP, 32:35], t.hot[:, j, NG * P:], t.bring[:, j, bass.ds(e, 1), 0:3].rearrange("p a n -> p (a n)"),
                                   start=(j == 0), stop=(j == TT - 1), tile_position=(0, 0))
                mm.then_inc(t.s_disp, 1)

            def spread_bias(i):
                pe.wait_ge(t.s_pick, i + 1)
                for half in range(2):
                    mm = pe.matmul(bank[PY[half]][:, FC:], t.pick[:, :], t.b1all[:, half * FC:(half + 1) * FC], start=True, stop=True)
                mm.then_inc(t.s_spread, 1)

            def turn(i):
                pe.wait_ge(t.s_gather, i * 16 + 16)
                for c in range(2):
                    for x in range(4):
                        k = 4 * c + x
                        mm = pe.transpose(bank[PX[c]][:, x * CAP:(x + 1) * CAP], t.xg[:, k * P:(k + 1) * P], ident[0:CAP, 0:CAP])
                    mm.then_inc(t.s_xt, 1)

            def up(k, g):
                for c in range(4):
                    cols = t.w1[:, k, :].rearrange("p (a n) -> p a n", a=2)[:, :, c * FC:(c + 1) * FC]
                    mm = pe.matmul(halves(bank[g][c * G:(c + 1) * G, :], FC), t.xe[:, k, g * G:(g + 1) * G], cols,
                                   start=(k == 0), stop=(k == KB - 1), tile_position=(0, c * G))
                return mm

            def turn_act(i, g):
                pe.wait_ge(t.s_a, i * NG + g + 1)
                for x in range(2):
                    mm = pe.transpose(bank[PT[g]][:, x * P:(x + 1) * P], t.a[:, g, x * P:(x + 1) * P], ident)
                mm.then_inc(t.s_at, 1)

            def down(i, g, last, side):
                pe.wait_ge(t.s_ae, i * NG + g + 2)
                pe.wait_ge(t.s_ysb, i * NG + (2 if g == 2 else 1))
                if g == 0:
                    pe.wait_ge(t.s_b1, i * 2 + 2)
                    for b in range(4):
                        pe.wait_ge(t.s_w2[b], i * 16 + 16)
                for b in range(4):
                    for x in range(2):
                        for c in range(4):
                            mm = pe.matmul(bank[PY[g % 2]][c * G:(c + 1) * G, 0:FC], t.aT[:, g, x, b * G:(b + 1) * G], t.w2p[:, side, b, x, c * FC:(c + 1) * FC],
                                           start=(b == 0 and x == 0), stop=(b == 3 and x == 1), tile_position=(0, c * G))
                    if g == last:
                        mm.then_inc(t.s_w2used, 1)
                if g < last:
                    mm.then_inc(t.s_y, 1)

            def work(i, groups, side):
                last = groups - 1
                for k in range(K_EACH):
                    pe.wait_ge(t.s_w1[k], i * 16 + 16)
                    for g in range(groups):
                        mm = up(k, g)
                    mm.then_inc(t.s_w1used, 1)
                    if k == 0:
                        pe.wait_ge(t.s_slots, i + 1)
                        pe.wait_ge(t.s_ysb, i * NG + 1)
                        dispatch(i + 1)
                        spread_bias(i)
                for g in range(groups):
                    for k in range(K_EACH, KB):
                        if g == 0:
                            pe.wait_ge(t.s_w1[k], i * 16 + 16)
                        mm = up(k, g)
                        if g == last:
                            mm.then_inc(t.s_w1used, 1)
                    if g < last:
                        mm.then_inc(t.s_up, 1)
                if groups < NG:
                    pe.wait_ge(t.s_w1used, i * KB + KB)
                    pe.sem_inc(t.s_up, 1)
                pe.wait_ge(t.s_slots, i + 2)
                turn_act(i, 0)
                turn(i + 1)
                turn_act(i, 1)
                down(i, 0, last, side)
                if groups == NG:
                    turn_act(i, 2)
                else:
                    pe.wait_ge(t.s_ae, i * NG + 3)
                    pe.sem_inc(t.s_at, 1)
                down(i, 1, last, side)
                if groups == NG:
                    down(i, 2, last, side)
                else:
                    pe.wait_ge(t.s_w2used, i * 4 + 4)
                    pe.sem_inc(t.s_y, 1)

            dispatch(0)
            for x in range(TT, 2 * TT):
                if x >= TT + 2:
                    pe.wait_ge(t.s_acc, x - TT - 1)
                gated_bias(pe, t, x)
            pe.wait_ge(t.s_acc, TT)
            turn(0)
            pe.wait_ge(t.s_acc, 2 * TT)
            with pe.Fori(0, pairs) as r:
                for side in range(2):
                    i = r * 2 + side
                    pe.wait_ge(t.s_xe, i * 2 + 2)
                    pe.wait_ge(t.s_hfree, i * NG + NG)
                    pe.wait_ge(t.s_ae, i * NG + 1)
                    tokens = pe.value_load(t.lists[0:1, bass.ds(i + 2 * P, 1)], min_val=0, max_val=SEQ)
                    with pe.If(tokens > (NG - 1) * G):
                        work(i, NG, side)
                    with pe.Else():
                        work(i, NG - 1, side)

        @block.vector
        def _(dve):
            n = pair_count(dve) * 2
            dve.sem_inc(t.s_hfree, NG)
            dve.sem_inc(t.s_ysb, 1)
            dve.sem_inc(t.s_ae, 1)

            def find(i, chain, base):
                e = expert_of(dve, i)
                for j in range(TT):
                    ins = dve.tensor_scalar(t.hot[:, j, :], t.kb[:, B_SLOT:B_SLOT + HOT], t.first[:, bass.ds(i, 1)],
                                            t.place[:, j, bass.ds(e, 1)], ALU.add, ALU.is_equal)
                    if j < TT - 1:
                        chain.add(ins)
                chain.sync(0, base)
                ins.then_inc(t.s_hot, 1)

            def slots(i, chain, base):
                dve.wait_ge(t.s_disp, i + 1)
                chain.add(dve.tensor_copy(t.slot[:, :, :], bank[5][:, 0:24].rearrange("p (a n) -> p a n", n=8)[:, :, 0:6]))
                dve.tensor_copy(t.rowf[:, 0:2], bank[5][0:CAP, 32:34]).then_inc(t.s_slots, 1)
                chain.sync(0, base)
                dve.wait_ge(t.s_slots, i + 2)
                q, r, one = (t.slot[:, :, c] for c in range(3))
                chain.add(dve.tensor_tensor(t.rowf[:, 2:3], t.rowf[:, 0:1], t.rowf[:, 1:2], ALU.add))
                chain.add(dve.tensor_tensor(q, q, r, ALU.add))
                chain.link(dve.tensor_tensor(one, one, t.kf[:, K_PAD:K_PAD + NG], ALU.mult), base)
                dve.tensor_scalar(t.gidx[:, :], t.rowf[:, 2:3], 0.25, None, ALU.mult).then_inc(t.s_gidx, 1)
                chain.add(dve.tensor_tensor(q, q, t.kf[:, K_ROW:K_ROW + NG], ALU.add))
                chain.link(dve.tensor_tensor(t.slot[:, :, 3], t.slot[:, :, 3], t.slot[:, :, 4], ALU.add), base)
                chain.link(dve.tensor_tensor(t.srow[:, bass.ds(i * NG, NG)], q, one, ALU.add), base)
                chain.link(dve.tensor_tensor(t.sgate[:, bass.ds(i * NG, NG)], t.slot[:, :, 3], t.slot[:, :, 5], ALU.add), base)

            def pick(i):
                e = expert_of(dve, i)
                dve.tensor_copy(halves(t.pick[:, :], G), t.kf[:, bass.ds(e * 4 + K_ID, 4)].unsqueeze(2).to_broadcast([P, 4, G])).then_inc(t.s_pick, 1)

            def turn(i):
                dve.wait_ge(t.s_xt, i * 2 + 2)
                dve.tensor_copy(t.xe[:, 4:8, :], halves(bank[PX[1]][:, 0:4 * CAP], CAP)).then_inc(t.s_xe, 1)

            def gated(i, g, chain, base):
                if g < NG - 1:
                    dve.wait_ge(t.s_up, i * (NG - 1) + g + 1)
                else:
                    dve.wait_ge(t.s_w1used, i * KB + KB)
                if g == 0:
                    dve.wait_ge(t.s_b1, i * 2 + 2)
                dve.tensor_tensor(t.hb[:, g, :], bank[g][:, :], t.b1[:, :], ALU.add).then_inc(t.s_hfree, 1)
                dve.wait_ge(t.s_hfree, i * NG + g + 1 + NG)
                dve.tensor_scalar(t.hb[:, g, 0:FC], t.hb[:, g, 0:FC], LIMIT, None, ALU.min).then_inc(t.s_glu, 1)
                chain.link(dve.tensor_scalar(t.hb[:, g, FC:], t.hb[:, g, FC:], LIMIT, -LIMIT, ALU.min, ALU.max), base)
                dve.wait_ge(t.s_glu, i * NG + g + 1)
                chain.link(dve.scalar_tensor_tensor(t.a[:, g, :], t.hb[:, g, FC:], 1.0, t.hb[:, g, 0:FC], ALU.add, ALU.mult), base)

            def swiglu(i, g):
                dve.wait_ge(t.s_sig, i * NG + g + 1)
                dve.tensor_tensor(t.a[:, g, :], t.a[:, g, :], t.sig[:, g, :], ALU.mult).then_inc(t.s_a, 1)

            def turned(i, g):
                dve.wait_ge(t.s_at, i * NG + g + 1)
                dve.tensor_copy(t.aT[:, g, :, :], halves(bank[PT[g]][:, 0:2 * P], P)).then_inc(t.s_ae, 1)

            pre = Chain(dve, t.s_pre)
            pick(0)
            dve.sem_inc(t.s_slots, 1)
            find(0, pre, 0)
            slots(0, pre, 0)
            for x in range(2 * TT):
                j, c, b = bias_part(x)
                half = t.h[:, j, c * SEQ:(c + 1) * SEQ]
                dve.wait_ge(t.s_bias, x + 1)
                dve.tensor_tensor(half, half, bank[b][:, :], ALU.add).then_inc(t.s_acc, 1)
            turn(0)
            STEPS = 3 + 8 + 2 * NG
            with dve.Fori(0, n) as i:
                step, base = Chain(dve, t.s_step), i * STEPS
                find(i + 1, step, base)
                slots(i + 1, step, base)
                dve.wait_ge(t.s_spread, i + 1)
                dve.sem_inc(t.s_passed, 1)
                pick(i + 1)
                dve.wait_ge(t.s_scat, i * 48 + 48)
                dve.tensor_copy(t.sidx[:, :], t.srow[:, bass.ds(i * NG, NG)]).then_inc(t.s_sidx, 1)
                for g in range(2):
                    gated(i, g, step, base)
                    swiglu(i, g)
                turned(i, 0)
                gated(i, 2, step, base)
                turn(i + 1)
                turned(i, 1)
                swiglu(i, 2)
                turned(i, 2)
                assert step.n == STEPS, step.n


def finish(nc, t):
    with nc.Block() as block:

        @block.sync
        def _(sp):
            for j in range(TT):
                sp.dma_start(t.h[:, j, :], t.d_acc[j * P:(j + 1) * P, :]).then_inc(t.s_hin[j], 16)
            for j in range(TT):
                sp.wait_ge(t.s_res, j + 1)
                sp.dma_start(t.out[j * P:(j + 1) * P, :], t.u2[:, j, :]).then_inc(t.s_out, 16)
            sp.wait_ge(t.s_out, 16 * TT)

        @block.scalar
        def _(act):
            act.activation(t.nv1[:, 0:1], t.eps[:, 0:1], ACT.Sqrt).then_inc(t.s_froot, 1)
            for j in range(TT):
                act.wait_ge(t.s_hin[j], 16)
                act.activation(t.u2[:, j, :], t.h[:, j, :], ACT.Square, accum_out=t.ss[:, j:j + 1]).then_inc(t.s_fss, 1)
                act.wait_ge(t.s_fss, j + 1)
                act.activation(t.ss[:, j:j + 1], t.ss[:, j:j + 1], ACT.Sqrt, bias=t.eps[:, 0:1], scale=1.0 / D).then_inc(t.s_froot, 1)

        @block.vector
        def _(dve):
            dve.wait_ge(t.s_fin, 16)
            for j in range(TT):
                dve.wait_ge(t.s_froot, j + 2)
                dve.reciprocal(t.ss[:, j:j + 1], t.ss[:, j:j + 1]).then_inc(t.s_frec, 1)
                dve.wait_ge(t.s_frec, j + 1)
                dve.scalar_tensor_tensor(t.u2[:, j, :], t.h[:, j, :], t.ss[:, j:j + 1], t.gfin[:, :], ALU.mult, ALU.mult).then_inc(t.s_res, 1)


def build(nc, io):
    with ExitStack() as ctx:
        t = Tensors()
        t.d_kf = io["d_kf"]
        t.d_kb = io["d_kb"]
        t.d_dense = io["d_dense"]
        t.d_chan = io["d_chan"]
        t.d_x = io["d_x"]
        t.d_xT = io["d_xT"]
        t.d_pos = io["d_pos"]
        t.d_sinks = io["d_sinks"]
        t.d_wr = io["d_wr"]
        t.d_gffn = io["d_gffn"]
        t.d_gfin = io["d_gfin"]
        t.d_b2 = io["d_b2"]
        t.d_b1 = io["d_b1"]
        t.d_w1 = io["d_w1"]
        t.d_w2 = io["d_w2"]
        t.out = io["out"]

        def sb(name, shape, dt=F32):
            return ctx.enter_context(nc.sbuf_tensor(name, shape, dt))

        def rounded(name, shape):
            tensor = sb(name, shape)
            place = nc.sbuf_base - 4 * shape[1]
            return tensor, nc.alloc_sbuf_tensor_at(name + "_r", tuple(shape), F32R, offset=place)

        def sem(name):
            return ctx.enter_context(nc.semaphore(name))

        def sems(name, n):
            return [sem(f"{name}_{i}") for i in range(n)]

        t.d_acc = nc.dram_tensor("acc", (SEQ + P, D), F32, kind="Internal").ap()
        t.d_acc4 = t.d_acc.rearrange("r (c n) -> (r c) n", n=FC)
        t.d_u2 = nc.dram_tensor("u2_rows", (SEQ, D), F32, kind="Internal").ap()

        big, big_r = rounded("big", [P, 24576])
        t.w1 = big[:, 0:16384].rearrange("p (k n) -> p k n", k=KB)
        w2_place = nc.sbuf_base - 4 * 8192
        t.qT = halves(big[:, 0:4096], SEQ)
        t.gates = halves(big[:, 4096:12288], SEQ)
        t.cT = halves(big[:, 12288:12288 + KB * CW], CW)
        t.cv = halves(big[:, 16640:20736], SEQ)
        t.kT = halves(big[:, 20736:22016], SEQ + WIN)
        t.v = halves(big[:, 22016:22656], P)
        t.vT = big[:, 22656:23168]
        t.csum = big[:, 23168:24192].rearrange("p (a n) -> p a n", n=512)
        t.cv_hi = t.mix_hi = halves(big_r[:, 12288:16384], SEQ)
        t.cv_lo = halves(big_r[:, 16640:20736], SEQ)
        xT, xT_r = rounded("xT", [P, 4096])
        t.xT = halves(xT[:, :], SEQ)
        t.u2 = halves(xT[:, :], D)
        t.o_lo = halves(xT_r[:, :], SEQ)
        uT, uT_r = rounded("uT", [P, 4096])
        t.uT = halves(uT[:, :], SEQ)
        t.h = halves(uT[:, :], D)
        t.o_hi = t.u_lo = halves(uT_r[:, :], SEQ)
        w2_pair = nc.alloc_sbuf_tensor_at("w2_pair", (P, 16384), F32, offset=w2_place)
        assert nc.sbuf_base == w2_place + 4 * 16384
        t.w2p = w2_pair[:, :].rearrange("p (s j a n) -> p s j a n", s=2, j=4, a=2)
        t.w2 = t.w2p[:, 0]
        ring, ring_r = rounded("ring", [P, 4096])
        t.wring, t.wlo = halves(ring[:, :], D), halves(ring_r[:, :], D)
        t.xg = ring[0:CAP, 0:1024]
        t.xe = halves(ring[:, 1024:1792], CAP)
        t.hb = halves(ring[:, 1792:3328], 2 * FC)
        t.sig = halves(ring[:, 3328:4096], FC)
        mix, mix_r = rounded("mix", [P, 4096])
        t.mix = t.u2T = halves(mix[:, :], SEQ)
        t.u_hi = t.mix_lo = halves(mix_r[:, :], SEQ)
        t.a = halves(mix[:, 0:768], FC)
        t.aT = mix[:, 768:1536].rearrange("p (g x n) -> p g x n", g=NG, x=2)
        t.ysb = halves(mix[:, 1536:2304], FC)
        t.hot = halves(mix[:, 2304:2304 + TT * HOT // 2].bitcast(BF16), HOT)
        sm, sm_r = rounded("sm", [P, 2048])
        t.sm = sm[:, :].rearrange("p (u x n) -> p u x n", u=2, x=4)
        t.gffn, t.b2 = sm[:, 0:1024], sm[:, 1024:2048]
        t.gfin = t.gffn
        t.hi_early = (sm_r[:, 0:1024], sm_r[:, 1024:2048])
        pT = sb("pT", [P, 1024])
        t.pT, t.b1all = pT[:, :].rearrange("p (k x n) -> p k x n", k=2, x=4), pT[:, 0:2 * FC]
        rope, rope_r = rounded("rope", [P, 1024])
        t.sin, t.cos, t.kb32 = rope[:, 0:512], rope[:, 512:1024], rope[:, 0:B_W]
        angles, angles_r = rounded("angles", [P, 1024])
        t.ang, t.pos_i, t.zrow = angles[:, 0:512], angles[:, 512:1024].bitcast(I32), angles[:, :]
        t.xcos = halves(angles[:, :], 512)
        t.hi_late = (rope_r[:, :], angles_r[:, :])
        t.rstd, t.odd, t.b1 = (sb(x, [P, 512]) for x in ("rstd", "odd", "b1"))
        t.kf, t.kb, t.chan = sb("kf", [P, K_W]), sb("kb", [P, B_W], BF16), sb("chan", [P, V_W])
        t.sinks, t.wr, t.eps = sb("sinks_sb", [P, HEADS]), sb("wr", [P, KB * E]), sb("eps", [P, 1])
        t.negm, t.rsum, t.esink, t.mx = (sb(x, [P, NU, 4]) for x in ("negm", "rsum", "esink", "mx"))
        t.ss, t.nv1, t.room = (sb(x, [P, TT]) for x in ("ss", "nv1", "room"))
        t.lT, t.diag, t.first = (sb(x, [P, P]) for x in ("lT", "diag", "first"))
        t.gT = halves(t.odd[:, :], P)
        t.pick = t.lT
        t.logits, t.sel, t.tie, t.rank, t.gexp, t.gate, t.place = (
            sb(x, [P, TT, E]) for x in ("logits", "sel", "tie", "rank", "gexp", "gate", "place"))
        t.selb, t.top = sb("selb", [P, TT, E], BF16), sb("top", [P, TT, 8])
        t.cnt, t.more, t.run, t.below = (sb(x, [P, E]) for x in ("cnt", "more", "run", "below"))
        t.tmp, t.listcol, t.lists = sb("tmp", [P, 4]), sb("listcol", [P, LIST]), sb("lists", [1, LIST * P], I32)
        t.bring = sb("bring", [P, TT, E, 6], BF16)
        t.slot, t.rowf, t.gidx, t.sidx = sb("slot", [P, NG, 6]), sb("rowf", [CAP, 3]), sb("gidx", [CAP, 1], I32), sb("sidx", [P, NG], I32)
        t.srow, t.sgate = sb("srow", [P, NG * 64]), sb("sgate", [P, NG * 64])
        t.bank = [ctx.enter_context(nc.psum_tensor(f"bank{i}", [P, 512], F32)) for i in range(8)]

        t.s_const = sem("s_const")
        t.s_kf = sem("s_kf")
        t.s_sq = sem("s_sq")
        t.s_sqodd = sem("s_sqodd")
        t.s_csum = sem("s_csum")
        t.s_lnsq = sem("s_lnsq")
        t.s_whi = sem("s_whi")
        t.s_wlo = sem("s_wlo")
        t.s_hi = sem("s_hi")
        t.s_lo = sem("s_lo")
        t.s_olo = sem("s_olo")
        t.s_vt = sem("s_vt")
        t.s_v = sem("s_v")
        t.s_stat = sem("s_stat")
        t.s_eps = sem("s_eps")
        t.s_root = sem("s_root")
        t.s_ang = sem("s_ang")
        t.s_rope = sem("s_rope")
        t.s_prod = sem("s_prod")
        t.s_evac = sem("s_evac")
        t.s_gated = sem("s_gated")
        t.s_cent = sem("s_cent")
        t.s_lnt = sem("s_lnt")
        t.s_lns = sem("s_lns")
        t.s_ln = sem("s_ln")
        t.s_max = sem("s_max")
        t.s_exp = sem("s_exp")
        t.s_pt = sem("s_pt")
        t.s_pv = sem("s_pv")
        t.s_ept0 = sem("s_ept0")
        t.s_ept1 = sem("s_ept1")
        t.s_eo = sem("s_eo")
        t.s_late = sem("s_late")
        t.s_h = sem("s_h")
        t.s_ss = sem("s_ss")
        t.s_ut = sem("s_ut")
        t.s_eut0 = sem("s_eut0")
        t.s_eut1 = sem("s_eut1")
        t.s_top = sem("s_top")
        t.s_gexp = sem("s_gexp")
        t.s_uT = sem("s_uT")
        t.s_rot = sem("s_rot")
        t.s_swap = sem("s_swap")
        t.s_conv = sem("s_conv")
        t.s_masked = sem("s_masked")
        t.s_score = sem("s_score")
        t.s_prob = sem("s_prob")
        t.s_merge = sem("s_merge")
        t.s_u2 = sem("s_u2")
        t.s_route = sem("s_route")
        t.s_lt = sem("s_lt")
        t.s_sel = sem("s_sel")
        t.s_gate = sem("s_gate")
        t.s_gT = sem("s_gT")
        t.s_acc = sem("s_acc")
        t.s_bias = sem("s_bias")
        t.s_diag = sem("s_diag")
        t.s_first = sem("s_first")
        t.s_efirst = sem("s_efirst")
        t.s_dve = sem("s_dve")
        t.s_tap = sem("s_tap")
        t.s_zero = sem("s_zero")
        t.s_scat = sem("s_scat")
        t.s_x = sem("s_x")
        t.s_u2out = sem("s_u2out")
        t.s_list = sem("s_list")
        t.s_listrow = sem("s_listrow")
        t.s_rows = sem("s_rows")
        t.s_xcos = sem("s_xcos")
        t.s_lna = sem("s_lna")
        t.s_accout = sem("s_accout")
        t.s_w1used = sem("s_w1used")
        t.s_w2used = sem("s_w2used")
        t.s_gather = sem("s_gather")
        t.s_gidx = sem("s_gidx")
        t.s_xt = sem("s_xt")
        t.s_ysb = sem("s_ysb")
        t.s_sidx = sem("s_sidx")
        t.s_xe = sem("s_xe")
        t.s_pick = sem("s_pick")
        t.s_b1 = sem("s_b1")
        t.s_spread = sem("s_spread")
        t.s_passed = sem("s_passed")
        t.s_glu = sem("s_glu")
        t.s_sig = sem("s_sig")
        t.s_y = sem("s_y")
        t.s_hot = sem("s_hot")
        t.s_disp = sem("s_disp")
        t.s_a = sem("s_a")
        t.s_at = sem("s_at")
        t.s_ae = sem("s_ae")
        t.s_hfree = sem("s_hfree")
        t.s_up = sem("s_up")
        t.s_slots = sem("s_slots")
        t.s_pre = sem("s_pre")
        t.s_step = sem("s_step")
        t.s_go = sem("s_go")
        t.s_fin = sem("s_fin")
        t.s_res = sem("s_res")
        t.s_out = sem("s_out")
        t.s_fss = sem("s_fss")
        t.s_froot = sem("s_froot")
        t.s_frec = sem("s_frec")
        t.s_xT = sems("s_xT", 4)
        t.s_w = sems("s_w", NSLOT)
        t.s_w1 = sems("s_w1", KB)
        t.s_w2 = sems("s_w2", 4)
        t.s_hin = sems("s_hin", TT)

        dense_half(nc, t)
        mixture(nc, t)
        finish(nc, t)


def constants():
    p = np.arange(P)
    kf = np.zeros((P, K_W), np.float32)
    kf[:, K_ID:K_ID + P] = np.eye(P)
    kf[:, K_MEAN:K_MEAN + P] = 1.0 / D
    kf[:, K_ONE:K_ONE + P] = 1.0
    rot = HD // 8
    for head in range(2):
        for d in range(rot):
            kf[head * HD + d + rot, K_ROT + head * HD + d] = -1.0
            kf[head * HD + d, K_ROT + head * HD + d + rot] = 1.0
            freq = np.float32(500000.0) ** np.float32(-2.0 * d / (2 * rot))
            kf[head * HD + d, K_FREQ] = kf[head * HD + d + rot, K_FREQ] = freq
    q, k = np.arange(WIN)[:, None] + WIN, np.arange(2 * WIN)[None, :]
    band = (q - k >= 0) & (q - k < WIN)
    kf[:, K_MASK:K_MASK + 256] = np.where(band, 0.0, MASKED)
    kf[:, K_MASK + 256:K_MASK + 512] = np.where(band & (k >= WIN), 0.0, MASKED)
    kf[:, K_HALFPI] = np.pi / 2
    tile, token = p // G, p % G
    kf[:, K_TILE:K_TILE + TT] = p[:, None] // E == np.arange(TT)
    for g in range(NG):
        pad = 4 * (SEQ + g * G + token)
        kf[:, K_PAD + g] = -pad
        kf[:, K_ROW + g] = pad + tile
    kf[:, K_P] = p
    kf[:, K_E:K_E + E] = np.arange(E)
    kb = np.zeros((P, B_W), np.float32)
    kb[:, B_TRI:B_TRI + P] = p[:, None] < p[None, :]
    kb[:, B_ONE:B_ONE + P] = 1.0
    for g in range(NG):
        kb[:, B_SLOT + g * P:B_SLOT + (g + 1) * P] = g * G + token[None, :]
    kb[:, B_SLOT + NG * P:B_SLOT + HOT] = np.arange(CAP)
    for j in range(TT):
        kb[:, B_TOK + 3 * j:B_TOK + 3 * j + 3] = np.stack([np.full(P, 4 * P * j), 4 * p, np.ones(P)], 1)
    return kf, kb


def lay_out(a):
    def blocks(w):
        n = w.shape[1] // P
        return w.reshape(KB, P, n, P).transpose(2, 1, 0, 3).reshape(n, P, KB * P)

    def by_channel(v):
        return v.reshape(KB, P).T

    w_in = a["w_in"][0]
    conv_value, conv_gate, wq, wk, wv, gates = np.split(w_in, np.cumsum([D, D, D, KV * HD, KV * HD]), axis=1)
    pairs = np.stack([blocks(conv_value), blocks(conv_gate)], 1).reshape(16, P, D)
    twice = np.concatenate([wk[:, 0:HD], wk[:, 0:HD], wk[:, HD:], wk[:, HD:]], 1)
    dense = np.concatenate([
        pairs, blocks(wq), blocks(twice), blocks(wv), np.zeros((1, P, D), np.float32), blocks(gates),
        blocks(a["w_conv_out"][0]), blocks(a["w_attn_out"][0]), a["w_out"][0].reshape(KB, P, D)])
    kf, kb = constants()
    w_dw = a["w_dw"][0].reshape(TAPS, KB, P).transpose(2, 1, 0).reshape(P, KB * TAPS)
    router_bias = np.tile(a["b_router"][0], TT).reshape(P, 1)
    chan = np.concatenate([w_dw] + [by_channel(a[x][0]) for x in ("b_dw", "g_conv_ln", "b_conv_ln", "g_mix_norm")] + [router_bias], 1)
    sinks = a["attn_sinks"][0].reshape(4, 2, 2).transpose(0, 2, 1).reshape(HEADS)
    b1 = a["b_mlp1"][0].reshape(E, 2, 4, FC).transpose(0, 2, 1, 3).reshape(4 * E, 2 * FC)
    return {
        "d_kf": kf, "d_kb": kb, "d_dense": dense, "d_chan": chan,
        "d_x": a["x"][0], "d_xT": a["x"][0].T.reshape(KB, P, SEQ).transpose(1, 0, 2),
        "d_pos": a["positions"].astype(np.int32).reshape(SEQ), "d_sinks": sinks,
        "d_wr": a["w_router"][0].reshape(KB, P, E).transpose(1, 0, 2).reshape(P, KB * E),
        "d_gffn": a["g_ffn_norm"][0], "d_gfin": a["g_final"],
        "d_b2": np.tile(a["b_mlp2"][0], (TT, 1)), "d_b1": b1,
        "d_w1": a["w_mlp1"][0], "d_w2": a["w_mlp2"][0],
    }


def kernel(**inputs):
    import concourse.bacc as bacc
    from concourse.bass_utils import run_bass_kernel_spmd as run

    arrays = {k: np.ascontiguousarray(v) for k, v in lay_out({k: np.asarray(v) for k, v in inputs.items()}).items()}
    nc = bacc.Bacc("TRN2", target_bir_lowering=False, num_devices=1)
    io = {name: nc.dram_tensor(f"in_{name}", x.shape, mybir.dt.from_np(x.dtype), kind="ExternalInput").ap() for name, x in arrays.items()}
    io["out"] = nc.dram_tensor("out_rows", (SEQ, D), F32, kind="ExternalOutput").ap()
    build(nc, io)
    r = run(nc, [{f"in_{k}": v for k, v in arrays.items()}], core_ids=[0])
    return r.results[0]["out_rows"].reshape(1, SEQ, D)
```
